# Optimizing a Trainium2 kernel written in Bass

```python
import math
import jax
import jax.numpy as jnp
from jax import lax
import numpy as np

D_MODEL = 1024
BATCH = 1
SEQ = 512
DEPTH = 2

A_HEADS = 4
A_NOPE = 64
A_ROPE = 32
A_V = 64
Q_LORA = 192
KV_LORA = 128
ROPE_THETA = 10000.0
B_HEADS = 4
B_DIM = 64
DILATED_PATTERNS = ((128, 1), (512, 4), (2048, 16))
DIL_BLOCK = 128
C_HEADS = 4
C_DIM = 64
IDX_HEADS = 8
IDX_DIM = 32
IDX_TOPK_MAX = 256
D_HEADS = 4
D_QK = 32
D_V = 64
BRANCH_WIDTH = 256
MIX_WIDTH = 4 * BRANCH_WIDTH
NUM_BUCKETS = 32
MAX_DISTANCE = 2048
BIAS_HEADS = B_HEADS + C_HEADS + D_HEADS
Q_BLOCK = 128
NEG_INF = -1e30
EPS = 1e-6
SPLIT_SIZES = (
    Q_LORA, KV_LORA, A_ROPE, BRANCH_WIDTH,
    BRANCH_WIDTH, BRANCH_WIDTH, BRANCH_WIDTH, BRANCH_WIDTH,
    BRANCH_WIDTH, BRANCH_WIDTH, BRANCH_WIDTH, IDX_HEADS * IDX_DIM, IDX_DIM, IDX_HEADS, BRANCH_WIDTH,
    2 * D_HEADS * D_QK, 2 * D_HEADS * D_QK, D_HEADS * D_V, BRANCH_WIDTH,
)
IN_COLS = sum(SPLIT_SIZES)

kernel_name = "hybrid_mla_dilated_dsa_diff_parallel_heads"

def rms_norm(x, g):
    xf = x.astype(jnp.float32)
    y = xf * lax.rsqrt(jnp.mean(xf * xf, axis=-1, keepdims=True) + EPS)
    return (y * g.astype(jnp.float32)).astype(x.dtype)

def t5_bucket(rel):
    n = jnp.maximum(rel, 0)
    max_exact = NUM_BUCKETS // 2
    nf = jnp.maximum(n, max_exact).astype(jnp.float32)
    large = max_exact + (jnp.log(nf / max_exact) / math.log(MAX_DISTANCE / max_exact)
                         * (NUM_BUCKETS - max_exact)).astype(jnp.int32)
    large = jnp.minimum(large, NUM_BUCKETS - 1)
    return jnp.where(n < max_exact, n, large)

def rope_tables(seq):
    inv = ROPE_THETA ** (-jnp.arange(0, A_ROPE, 2, dtype=jnp.float32) / A_ROPE)
    ang = jnp.arange(seq, dtype=jnp.float32)[:, None] * inv[None, :]
    return jnp.cos(ang), jnp.sin(ang)

def apply_rope(x, cos, sin):
    half = x.shape[-1] // 2
    x1, x2 = x[..., :half], x[..., half:]
    return jnp.concatenate([x1 * cos - x2 * sin, x1 * sin + x2 * cos], axis=-1).astype(x.dtype)

def to_blocks(a, nb):
    return jnp.moveaxis(a.reshape((a.shape[0], nb, Q_BLOCK) + a.shape[2:]), 1, 0)

def from_blocks(a):
    a = jnp.moveaxis(a, 0, 1)
    return a.reshape((a.shape[0], a.shape[1] * a.shape[2]) + a.shape[3:])

def mla_branch(c_q, c_kv, k_rope, q_norm, kv_norm, w_uq, w_ukv, cos, sin):
    bsz, seq, _ = c_q.shape
    q = (rms_norm(c_q, q_norm) @ w_uq).reshape(bsz, seq, A_HEADS, A_NOPE + A_ROPE)
    q_nope = q[..., :A_NOPE]
    q_rope = apply_rope(q[..., A_NOPE:], cos[:, None, :], sin[:, None, :])
    kv = (rms_norm(c_kv, kv_norm) @ w_ukv).reshape(bsz, seq, A_HEADS, A_NOPE + A_V)
    k_nope, v = kv[..., :A_NOPE], kv[..., A_NOPE:]
    k_rope = apply_rope(k_rope, cos, sin)
    scale = (A_NOPE + A_ROPE) ** -0.5
    keys = jnp.arange(seq)

    def block(args):
        qn, qr, t0 = args
        t = t0 + jnp.arange(Q_BLOCK)
        s = (jnp.einsum('bqhd,bshd->bhqs', qn, k_nope)
             + jnp.einsum('bqhd,bsd->bhqs', qr, k_rope)).astype(jnp.float32) * scale
        s = jnp.where(keys[None, :] <= t[:, None], s, NEG_INF)
        p = jax.nn.softmax(s, axis=-1).astype(v.dtype)
        return jnp.einsum('bhqs,bshd->bqhd', p, v)

    nb = seq // Q_BLOCK
    o = lax.map(block, (to_blocks(q_nope, nb), to_blocks(q_rope, nb), jnp.arange(nb) * Q_BLOCK))
    return from_blocks(o).reshape(bsz, seq, A_HEADS * A_V)

def dilated_pattern(q, k, v, table, window, dilation):
    bsz, seq, heads, dim = q.shape
    n = seq // dilation
    span = window // dilation
    blk = min(DIL_BLOCK, n)
    nb = -(-n // blk)
    n_pad = nb * blk

    def to_classes(a):
        a = jnp.swapaxes(a.reshape(bsz, n, dilation, heads, dim), 1, 2)
        a = jnp.pad(a, ((0, 0), (0, 0), (0, n_pad - n), (0, 0), (0, 0)))
        return a.reshape(bsz, dilation, nb, blk, heads, dim)

    def with_prev(a):
        prev = jnp.pad(a, ((0, 0), (0, 0), (1, 0), (0, 0), (0, 0), (0, 0)))[:, :, :-1]
        return jnp.concatenate([prev, a], axis=3)

    qc = to_classes(q)
    kc = with_prev(to_classes(k))
    vc = with_prev(to_classes(v))
    rel = jnp.arange(blk)[:, None] + blk - jnp.arange(2 * blk)[None, :]
    bias = jnp.transpose(table[t5_bucket(rel * dilation)], (0, 2, 1))
    in_band = ((rel >= 0) & (rel <= span))[None, :, None, :]
    has_prev = (jnp.arange(nb)[:, None, None, None] > 0) | (jnp.arange(2 * blk)[None, None, None, :] >= blk)
    mask = in_band & has_prev
    s = jnp.einsum('brnqhd,brnkhd->brnqhk', qc, kc).astype(jnp.float32) * (dim ** -0.5)
    s = jnp.where(mask, s + bias, NEG_INF)
    m = jnp.max(s, axis=-1)
    p = jnp.exp(s - m[..., None])
    l = jnp.sum(p, axis=-1)
    o = jnp.einsum('brnqhk,brnkhd->brnqhd', p, vc.astype(jnp.float32)) / l[..., None]

    def from_classes(a):
        a = a.reshape((bsz, dilation, n_pad) + a.shape[4:])[:, :, :n]
        return jnp.swapaxes(a, 1, 2).reshape((bsz, seq) + a.shape[3:])

    return from_classes(o), from_classes(m), from_classes(l)

def dilated_branch(q, k, v, table):
    bsz, seq, _ = q.shape
    q, k, v = (a.reshape(bsz, seq, B_HEADS, B_DIM) for a in (q, k, v))
    outs = [dilated_pattern(q, k, v, table, w, d) for (w, d) in DILATED_PATTERNS]
    o = jnp.stack([r[0] for r in outs])
    m = jnp.stack([r[1] for r in outs])
    l = jnp.stack([r[2] for r in outs])
    wts = l * jnp.exp(m - jnp.max(m, axis=0, keepdims=True))
    y = jnp.sum(wts[..., None] * o, axis=0) / jnp.sum(wts, axis=0)[..., None]
    return y.reshape(bsz, seq, BRANCH_WIDTH).astype(q.dtype)

def sparse_branch(q, k, v, q_idx, k_idx, w_idx, table, k_top):
    bsz, seq, _ = q.shape
    q = q.reshape(bsz, seq, C_HEADS, C_DIM)
    k = k.reshape(bsz, seq, C_HEADS, C_DIM)
    v = v.reshape(bsz, seq, C_HEADS, C_DIM)
    q_idx = q_idx.reshape(bsz, seq, IDX_HEADS, IDX_DIM)
    keys = jnp.arange(seq)
    gather = jax.vmap(lambda kb, ib: kb[ib])

    def block(args):
        qb, qib, wb, t0 = args
        t = t0 + jnp.arange(Q_BLOCK)
        logit = jnp.einsum('bqhd,bsd->bqhs', qib, k_idx).astype(jnp.float32) * (IDX_DIM ** -0.5)
        score = jnp.einsum('bqhs,bqh->bqs', jax.nn.relu(logit), wb.astype(jnp.float32)) * (IDX_HEADS ** -0.5)
        score = jnp.where(keys[None, None, :] <= t[None, :, None], score, NEG_INF)
        _, idx = lax.top_k(score, k_top)
        k_sel = gather(k, idx)
        v_sel = gather(v, idx)
        s = jnp.einsum('bqhd,bqkhd->bhqk', qb, k_sel).astype(jnp.float32) * (C_DIM ** -0.5)
        rel = t[None, :, None] - idx
        bias = jnp.transpose(table[t5_bucket(rel)], (0, 3, 1, 2))
        s = jnp.where((rel >= 0)[:, None], s + bias, NEG_INF)
        p = jax.nn.softmax(s, axis=-1).astype(v.dtype)
        return jnp.einsum('bhqk,bqkhd->bqhd', p, v_sel)

    nb = seq // Q_BLOCK
    o = lax.map(block, (to_blocks(q, nb), to_blocks(q_idx, nb), to_blocks(w_idx, nb),
                        jnp.arange(nb) * Q_BLOCK))
    return from_blocks(o).reshape(bsz, seq, BRANCH_WIDTH)

def diff_branch(q, k, v, lam_params, subln, table, lambda_init):
    bsz, seq, _ = q.shape
    q = q.reshape(bsz, seq, D_HEADS, 2, D_QK)
    k = k.reshape(bsz, seq, D_HEADS, 2, D_QK)
    v = v.reshape(bsz, seq, D_HEADS, D_V)
    lp = lam_params.astype(jnp.float32)
    lam = jnp.exp(jnp.sum(lp[0] * lp[1])) - jnp.exp(jnp.sum(lp[2] * lp[3])) + lambda_init
    keys = jnp.arange(seq)

    def block(args):
        qb, t0 = args
        t = t0 + jnp.arange(Q_BLOCK)
        s = jnp.einsum('bqhmd,bshmd->bmhqs', qb, k).astype(jnp.float32) * (D_QK ** -0.5)
        rel = t[:, None] - keys[None, :]
        bias = jnp.transpose(table[t5_bucket(rel)], (2, 0, 1))
        s = jnp.where(rel >= 0, s + bias, NEG_INF)
        p = jax.nn.softmax(s, axis=-1)
        a = p[:, 0] - lam * p[:, 1]
        return jnp.einsum('bhqs,bshd->bqhd', a.astype(v.dtype), v)

    nb = seq // Q_BLOCK
    o = from_blocks(lax.map(block, (to_blocks(q, nb), jnp.arange(nb) * Q_BLOCK)))
    o = rms_norm(o, subln) * (1.0 - lambda_init)
    return o.reshape(bsz, seq, BRANCH_WIDTH)

def setup_inputs(seed: int = 0) -> dict:
    key = jax.random.key(seed)
    ks = jax.random.split(key, 12)
    nrm = jax.random.normal
    return {
        "x": nrm(ks[0], (BATCH, SEQ, D_MODEL), jnp.float32),
        "w_in": nrm(ks[1], (DEPTH, D_MODEL, IN_COLS), jnp.float32) * D_MODEL ** -0.5,
        "w_out": nrm(ks[2], (DEPTH, MIX_WIDTH, D_MODEL), jnp.float32) * MIX_WIDTH ** -0.5,
        "norm_pre": 1.0 + 0.05 * nrm(ks[3], (DEPTH, D_MODEL), jnp.float32),
        "norm_post": 1.0 + 0.05 * nrm(ks[4], (DEPTH, D_MODEL), jnp.float32),
        "mla_q_norm": 1.0 + 0.05 * nrm(ks[5], (DEPTH, Q_LORA), jnp.float32),
        "mla_kv_norm": 1.0 + 0.05 * nrm(ks[6], (DEPTH, KV_LORA), jnp.float32),
        "mla_w_uq": nrm(ks[7], (DEPTH, Q_LORA, A_HEADS * (A_NOPE + A_ROPE)), jnp.float32) * Q_LORA ** -0.5,
        "mla_w_ukv": nrm(ks[8], (DEPTH, KV_LORA, A_HEADS * (A_NOPE + A_V)), jnp.float32) * KV_LORA ** -0.5,
        "diff_lambda": 0.1 * nrm(ks[9], (DEPTH, 4, D_QK), jnp.float32),
        "diff_subln": 1.0 + 0.05 * nrm(ks[10], (DEPTH, D_V), jnp.float32),
        "rel_bias": 0.5 * nrm(ks[11], (NUM_BUCKETS, BIAS_HEADS), jnp.float32),
    }

def reference(x, w_in, w_out, norm_pre, norm_post, mla_q_norm, mla_kv_norm, mla_w_uq, mla_w_ukv,
              diff_lambda, diff_subln, rel_bias):
    seq = x.shape[1]
    cos, sin = rope_tables(seq)
    k_top = min(IDX_TOPK_MAX, seq // 4)
    bias_b = rel_bias[:, :B_HEADS]
    bias_c = rel_bias[:, B_HEADS:B_HEADS + C_HEADS]
    bias_d = rel_bias[:, B_HEADS + C_HEADS:]
    split_at = np.cumsum(SPLIT_SIZES)[:-1].tolist()
    h = x
    for layer in range(DEPTH):
        u = rms_norm(h, norm_pre[layer])
        proj = u @ w_in[layer]
        (a_cq, a_ckv, a_kr, a_g,
         b_q, b_k, b_v, b_g,
         c_q, c_k, c_v, c_qi, c_ki, c_wi, c_g,
         d_q, d_k, d_v, d_g) = jnp.split(proj, split_at, axis=-1)
        y_a = mla_branch(a_cq, a_ckv, a_kr, mla_q_norm[layer], mla_kv_norm[layer],
                         mla_w_uq[layer], mla_w_ukv[layer], cos, sin) * jax.nn.silu(a_g)
        y_b = dilated_branch(b_q, b_k, b_v, bias_b) * jax.nn.silu(b_g)
        y_c = sparse_branch(c_q, c_k, c_v, c_qi, c_ki, c_wi, bias_c, k_top) * jax.nn.silu(c_g)
        lambda_init = 0.8 - 0.6 * math.exp(-0.3 * layer)
        y_d = diff_branch(d_q, d_k, d_v, diff_lambda[layer], diff_subln[layer], bias_d,
                          lambda_init) * jax.nn.silu(d_g)
        y = jnp.concatenate([y_a, y_b, y_c, y_d], axis=-1) @ w_out[layer]
        h = h + rms_norm(y, norm_post[layer])
    return h


_drawn_inputs = setup_inputs


def setup_inputs(seed=0):
    import zlib

    import numpy as np

    out = dict(_drawn_inputs(seed))
    spreads = {}
    factors = {'mla_q_norm': 3.823}
    for name, (base, spread) in spreads.items():
        noise = np.random.default_rng([zlib.crc32(name.encode()), seed]).standard_normal(out[name].shape)
        drawn = base * np.exp(spread * noise) if base else spread * noise
        out[name] = jnp.asarray(drawn.astype(out[name].dtype))
    for name, factor in factors.items():
        out[name] = (out[name] * factor).astype(out[name].dtype)
    return out
```

```python
from contextlib import ExitStack

import numpy as np

import concourse.bass as bass
from concourse import mybir

F32 = mybir.dt.float32
F32R = mybir.dt.float32r
ALU = mybir.AluOpType
ACT = mybir.ActivationFunctionType
AX_X = mybir.AxisListType.X

P = 128
DEPTH, SEQ, DM = 2, 512, 1024
NB = SEQ // P
KC = DM // P
HD = 64
HEADS = 4
A_QK, A_ROPE, QL, KVL = 96, 32, 192, 128
IDXH, DQK = 8, 32
TOPK = 128
NEG = -1e30
MARK = -3.0e38
EPS = 1e-6
BUCKETS = 32
TABLE_W = SEQ + P

OFF = {}
_at = 0
for _n, _w in (("cq", 192), ("ckv", 128), ("kr", 32), ("ga", 256), ("bq", 256), ("bk", 256), ("bv", 256),
               ("gb", 256), ("cqq", 256), ("ck", 256), ("cv", 256), ("qi", 256), ("ki", 32), ("wi", 8),
               ("gc", 256), ("dq", 256), ("dk", 256), ("dv", 256), ("gd", 256)):
    OFF[_n] = _at
    _at += _w
IN_COLS = _at

GROUPS = [
    ("cv", [(OFF["cv"], 256), (OFF["wi"], 8)], True),
    ("cq", [(OFF["cq"], 192), (OFF["kr"], 32), (OFF["ki"], 32)], False),
    ("qi", [(OFF["qi"], 256)], False),
    ("dq", [(OFF["dq"], 256)], False),
    ("dk", [(OFF["dk"], 256)], False),
    ("dv", [(OFF["dv"], 256)], True),
    ("gd", [(OFF["gd"], 256)], False),
    ("gc", [(OFF["gc"], 256)], False),
    ("ckv", [(OFF["ckv"], 128)], False),
    ("cqq", [(OFF["cqq"], 256)], False),
    ("ck", [(OFF["ck"], 256)], False),
    ("bq", [(OFF["bq"], 256)], False),
    ("bk", [(OFF["bk"], 256)], False),
    ("bv", [(OFF["bv"], 256)], True),
    ("gb", [(OFF["gb"], 256)], False),
    ("ga", [(OFF["ga"], 256)], False),
]
NGI = len(GROUPS)
NGO = 4
NG = NGI + NGO
GO_W = DM // NGO
GW = 264
GI = {g[0]: i for i, g in enumerate(GROUPS)}
WIDTH = [sum(w for _, w in g[1]) for g in GROUPS] + [GO_W] * NGO
SLOTS = 3
SEL_BLOCKS = (3, 2, 1)
N_CONSTS = 13
LAMBDA_STEPS = 3

JOBS = [(b, h) for b in "DCBA" for h in range(HEADS)]
NJ = len(JOBS)
WID = [P * (q + 1) for q in range(NB)]
POFF = [P * q * (q + 1) // 2 for q in range(NB)]
PACK = POFF[-1] + WID[-1]
TOFF = [sum(P * (NB - k) for k in range(kb)) for kb in range(NB)]


def layer_steps():
    st = [("u", tb) for tb in range(NB)]
    feat = lambda g, n=2: [("unit", g, c) for c in range(n)]
    tok = lambda g: [("unit", g, tb) for tb in range(NB)]
    st += tok("cv") + feat("cq") + feat("qi") + [("unit", "dq", 0)]
    st += [("idx", h) for h in range(4)] + [("unit", "dq", 1)] + [("idx", h) for h in range(4, 8)]
    st += [("topk", 0, 4)] + feat("dk", 1) + [("topk", 4, 10)] + [("unit", "dk", 1), ("topk", 10, 16)]
    for tb in range(NB):
        st += [("unit", "dv", tb), ("topk", 16 + 2 * tb, 18 + 2 * tb)]
    st += [("unit", "gd", 0), ("topk", 24, 28), ("unit", "gd", 1), ("topk", 28, 32)]
    extra = {
        0: [("topk", 32, 34)] + feat("gc") + [("topk", 34, 38)],
        1: [("topk", 38, 42)] + feat("ckv", 1) + [("topk", 42, 44)],
        2: feat("cqq") + [("topk", 44, 48), ("selmask",)],
        3: feat("ck"),
        4: feat("bq"),
        5: feat("bk"),
        6: tok("bv"),
        7: feat("gb"),
        8: feat("ga"),
        9: [("aup_head",)],
        10: [("aup", 0), ("aup", 1)],
        11: [("aup", 2), ("aup", 3)],
    }
    for j in range(NJ + 2):
        if j < NJ:
            st += [("scores", j)]
        st += extra.get(j, [])
        if j - 3 in (1, 3):
            st += [("dnorm", (j - 3) // 2)]
        st += [("mix", k) for k in {11: (6, 7), 12: (4, 5), 13: (2,), 14: (3,), 16: (0,)}.get(j, ())]
        if 0 <= j - 2:
            st += [("pv", j - 2)]
            if j - 2 in (1, 3):
                st += [("dsquares", (j - 2) // 2)]
        if 0 <= j - 1 < NJ:
            st += [("turn", j - 1)]
    st += [("mix", 1), ("out",)]
    return st


STEPS = layer_steps()


def units_of(step):
    k = step[0]
    if k == "u":
        return ["dve", "dve"]
    if k == "unit":
        if step[1] in ("cv", "dv", "bv", "ckv"):
            return ["act"]
        return ["act"] if step[1:] == ("cq", 0) else ["dve"]
    if k == "dnorm":
        return ["dve"]
    if k == "aup_head":
        return ["dve", "dve"]
    if k == "aup":
        return ["dve", "act", "act", "act"]
    return []


def highs_of(step):
    if step[0] == "u":
        return [True, True]
    if step[0] == "unit":
        return [units_of(step) == ["dve"]]
    return [False] * len(units_of(step))


UNIT_AT, UNIT_READER, UNIT_HIGH = {}, [], []
for _s in STEPS:
    UNIT_AT[_s] = len(UNIT_READER)
    UNIT_READER += units_of(_s)
    UNIT_HIGH += highs_of(_s)
NU = len(UNIT_READER)


def emptied(n, who):
    full, rest = divmod(n + 1, NU)
    return full * UNIT_READER.count(who) + UNIT_READER[:rest].count(who)


def highs(n):
    full, rest = divmod(n + 1, NU)
    return full * UNIT_HIGH.count(True) + UNIT_HIGH[:rest].count(True)


ROOTS = [("u", 0, tb) for tb in range(NB)]
for _l in range(DEPTH):
    ROOTS += [("d", _l, 0), ("d", _l, 1), ("a", _l, 0)]
    for _tb in range(NB):
        ROOTS += [("out", _l, _tb)] + ([("u", _l + 1, _tb)] if _l + 1 < DEPTH else [])
ROOT_AT = {r: i for i, r in enumerate(ROOTS)}

NS_IDX = IDXH * (NB - 1)
MAPS = [2 if b == "D" else 1 for b, _ in JOBS]
NSJ = NB * sum(MAPS)
S_AT = [NB * sum(MAPS[:j]) for j in range(NJ + 1)]
NS = NS_IDX + NSJ
STACKED = [("qi", 0), ("qi", 1), ("dq", 0), ("dq", 1), ("dk", 0), ("dk", 1)]
STACK_DMAS = 12
MIX_ORDER = [6, 7, 4, 5, 2, 3, 0, 1]


def probs_buffers(j):
    return [2 * (j % 2), 2 * (j % 2) + 1] if JOBS[j][0] == "D" else [j % 4]


def last_user(j):
    mine = set(probs_buffers(j))
    for i in range(j - 1, -1, -1):
        if mine & set(probs_buffers(i)):
            return i
    return None


def group_ended_by(step):
    if step[0] != "unit":
        return None
    _, cols, token = GROUPS[GI[step[1]]]
    last = NB - 1 if token else (sum(w for _, w in cols) + P - 1) // P - 1
    return GI[step[1]] if step[2] == last else None


LAST_UNIT = [UNIT_AT[s] for g in range(NGI) for s in STEPS if group_ended_by(s) == g]
def trunk(nc, x, w_in, w_out, norm_pre, norm_post, mla_q_norm, mla_kv_norm, mla_w_uq, mla_w_ukv,
          diff_lambda, diff_subln, rel_bias, onehot, headrows, rope_cc, rope_ss, ident_in, out):
    lam_init = [0.8 - 0.6 * float(np.exp(-0.3 * l)) for l in range(DEPTH)]
    h_dram = nc.dram_tensor("h_dram", [SEQ, DM], F32, kind="Internal").ap()
    strips_dram = nc.dram_tensor("strips_dram", [13, P, SEQ], F32, kind="Internal").ap()
    table_dram = nc.dram_tensor("table_dram", [13, TABLE_W], F32, kind="Internal").ap()

    with ExitStack() as ctx:
        base = (nc.sbuf_base + 63) // 64 * 64
        top = [base]
        arena = {}

        def room(name, nbytes):
            arena[name] = top[0]
            top[0] += (nbytes + 31) // 32 * 32
            assert top[0] <= nc.sbuf_usable_end, (name, top[0] - nc.sbuf_usable_end)

        def at(name, room_name, shape, dt, skip=0):
            return nc.alloc_sbuf_tensor_at(name, shape, dt, offset=arena[room_name] + skip)

        KB = 1024
        room("raw", SLOTS * KC * GW * 4)
        room("high", SLOTS * KC * GW * 4)
        room("uT", 32 * KB)
        room("gate", 16 * KB)
        for i in range(4):
            room(f"probs{i}", PACK * 4)
        for i in range(2):
            room(f"turned{i}", PACK * 4)
        room("values0", 4 * KB)
        room("values1", 4 * KB)
        room("X", 16 * KB)
        room("Y", 16 * KB)
        room("staging", 8 * KB)
        room("select", (PACK - P) * 4)
        room("kidx", 2 * KB)
        room("strips", 8 * KB)
        room("mask", 2 * KB)
        room("latent", 6 * KB)
        room("wukv", 2 * KB)
        room("od", 2 * KB)
        room("small", 5 * KB)
        w_raw = at("w_raw", "raw", [P, SLOTS, KC, GW], F32)
        w_low = at("w_low", "raw", [P, SLOTS, KC, GW], F32R)
        w_high = at("w_high", "high", [P, SLOTS, KC, GW], F32R)
        uT = at("uT", "uT", [P, 2, KC, SEQ], F32R)
        mix = at("mix", "uT", [P, 2, KC, SEQ], F32R)
        gate = at("gate", "gate", [P, KC, SEQ], F32)
        probs = [at(f"probs{i}", f"probs{i}", [P, PACK], F32) for i in range(4)]
        turned = [at(f"turned{i}", f"turned{i}", [P, PACK], F32) for i in range(2)]
        values = [at(f"values{i}", f"values{i}", [P, NB, HEADS * HD], F32) for i in range(2)]
        hX = at("hX", "X", [P, NB, DM], F32)
        qidx = at("qidx", "X", [P, IDXH, SEQ], F32R)
        dqk = [at(f"dqk{c}", "YX"[c], [P, 2, 4, SEQ], F32R) for c in range(2)]
        cqk = at("cqk", "Y", [P, 2, 2, 2, SEQ], F32R)
        bqk = at("bqk", "X", [P, 2, 2, 2, SEQ], F32R)
        aqk = at("aqk", "Y", [P, 2, HEADS, SEQ], F32)
        yg = at("yg", "Y", [P, NB, DM], F32)
        staging = at("staging", "staging", [P, 2, 2, SEQ], F32R)
        tokq = [at(f"tokq{i}", "staging", [P, HEADS, A_QK], F32, skip=1536 * i) for i in range(2)]
        tokk = [at(f"tokk{i}", "staging", [P, HEADS, A_QK], F32, skip=3072 + 1536 * i) for i in range(2)]
        ropet = at("ropet", "staging", [P, HEADS, A_ROPE], F32, skip=6144)
        kr = at("kr", "staging", [P, NB, A_ROPE], F32, skip=6656)
        kr2 = at("kr2", "staging", [P, NB, A_ROPE], F32, skip=7168)
        krx = at("krx", "staging", [P, NB, A_ROPE], F32, skip=7680)
        odsq = at("odsq", "staging", [P, NB, 2, HD], F32)
        sq = at("sq", "Y", [P, 3, SEQ], F32)
        od = at("od", "od", [P, NB, 2, HD], F32)
        tanh = at("tanh", "kidx", [P, SEQ], F32)
        select = at("select", "select", [P, PACK - P], F32)
        kidx = at("kidx", "kidx", [P, SEQ], F32R)
        strips = at("strips", "strips", [P, HEADS, SEQ], F32)
        mask = at("mask", "mask", [P, SEQ], F32)
        latq = at("latq", "latent", [P, 2, SEQ], F32)
        wuq = at("wuq", "select", [P, 2, HEADS * A_QK], F32)
        wukv = at("wukv", "wukv", [P, HEADS * P], F32)
        latkv = at("latkv", "latent", [P, SEQ], F32, skip=4 * KB)
        u = [at(f"u{i}", f"probs{i}", [P, DM], F32) for i in range(2)]
        waste = at("waste", "probs2", [P, DM], F32)
        gpre = at("gpre", "turned0", [P, DM], F32)
        gpost = at("gpost", "turned1", [P, DM], F32)
        u_in = [hX[:, t, :] for t in range(NB)]
        hot = at("hot", "Y", [34, TABLE_W], F32)
        heads13 = at("heads13", "Y", [34, 13], F32, skip=3 * KB)
        table = at("table", "Y", [13, TABLE_W], F32, skip=4 * KB)
        lamin = at("lamin", "Y", [P, DEPTH, 4, DQK], F32, skip=8 * KB)
        lampr = at("lampr", "Y", [P, DEPTH, 2, DQK], F32, skip=10 * KB)
        tiny_at = [arena["small"]]

        def tiny(name, shape):
            n = (4 * int(np.prod(shape[1:])) + 31) // 32 * 32
            t = nc.alloc_sbuf_tensor_at(name, shape, F32, offset=tiny_at[0])
            tiny_at[0] += n
            assert tiny_at[0] <= top[0]
            return t

        ident = tiny("ident", [P, P])
        cc = tiny("cc", [P, NB, A_ROPE])
        ss = tiny("ss", [P, NB, A_ROPE])
        wi = tiny("wi", [P, NB, IDXH])
        best = tiny("best", [P, 8])
        negmax = tiny("negmax", [P, 4, 2, NB])
        sums = tiny("sums", [P, 4, 2, NB])
        inv = tiny("inv", [P, 4, 2, NB])
        coef = tiny("coef", [P, 4, NB])
        sumsq = tiny("sumsq", [P, NB])
        ysq = tiny("ysq", [P, NB, 2])
        dsum = tiny("dsum", [P, 2 * NB])
        means = tiny("means", [P, 2, 8])
        roots = tiny("roots", [P, len(ROOTS), 8])
        minus_half = tiny("minus_half", [P, 8])
        ones = tiny("ones", [P, 1])
        lamdot = tiny("lamdot", [P, DEPTH, 2])
        neglam = tiny("neglam", [P, DEPTH])
        subln = tiny("subln", [P, DEPTH])
        gq = tiny("gq", [P, DEPTH, 2])
        gkv = tiny("gkv", [P, DEPTH])

        bank = ctx.enter_context(nc.psum_tensor("bank", [P, 8, 512], F32))
        WORK, SCORE, TURN, PV = 0, 2, 5, 7

        def sem(name):
            return ctx.enter_context(nc.semaphore(name))

        consts_loaded = sem("consts_loaded")
        table_ready, table_copied, table_stored = sem("table_ready"), sem("table_copied"), sem("table_stored")
        pool_ready, strips_stored = sem("pool_ready"), sem("strips_stored")
        strips_loaded = [sem(f"strips_loaded{h}") for h in range(HEADS)]
        mask_loaded = sem("mask_loaded")
        h_loaded = [sem(f"h_loaded{t}") for t in range(NB)]
        h_updated, h_stored = sem("h_updated"), sem("h_stored")
        gpre_loaded, gpost_loaded, a_loaded = sem("gpre_loaded"), sem("gpost_loaded"), sem("a_loaded")
        w_loaded = [sem(f"w_loaded{i}") for i in range(SLOTS)]
        w_high_done, w_low_done = sem("w_high_done"), sem("w_low_done")
        squares_summed, means_ready, roots_ready = sem("squares_summed"), sem("means_ready"), sem("roots_ready")
        u_ready = sem("u_ready")
        unit_ready, high_written = sem("unit_ready"), sem("high_written")
        emptied_by = {"act": sem("emptied_by_act"), "dve": sem("emptied_by_dve")}
        stack_loaded = [sem(f"stack_loaded{i}") for i in range(len(STACKED))]
        scores_ready, relu_done, index_added = sem("scores_ready"), sem("relu_done"), sem("index_added")
        select_done, bias_ready = sem("select_done"), sem("bias_ready")
        shifted, exp_done, probs_ready = sem("shifted"), sem("exp_done"), sem("probs_ready")
        turn_ready, turn_emptied = sem("turn_ready"), sem("turn_emptied")
        pv_ready, pv_emptied = sem("pv_ready"), sem("pv_emptied")
        od_ready, a_folded, lat_squared = sem("od_ready"), sem("a_folded"), sem("lat_squared")
        tokq_ready, kr_ready = sem("tokq_ready"), sem("kr_ready")
        mix_high, mix_low = sem("mix_high"), sem("mix_low")
        y_ready, y_squared, y_emptied = sem("y_ready"), sem("y_squared"), sem("y_emptied")
        vector_step, scalar_step, lam_exp = sem("vector_step"), sem("scalar_step"), sem("lam_exp")
        out_stored = sem("out_stored")

        def wait_unit_emptied(eng, n):
            who = UNIT_READER[n % NU]
            eng.wait_ge(emptied_by[who], emptied(n, who))

        def wait_w_loaded(eng, g):
            eng.wait_ge(w_loaded[g % SLOTS], 16 * sum(len(GROUPS[i % NG][1]) if i % NG < NGI else 1
                                                      for i in range(g % SLOTS, g + 1, SLOTS)))

        def wait_w_used(eng, g):
            l, i = divmod(g, NG)
            if i < NGI:
                eng.wait_ge(unit_ready, l * NU + LAST_UNIT[i] + 1)
            else:
                eng.wait_ge(y_ready, (l * NGO + i - NGI + 1) * NB)

        def jobs_scored(l, j):
            return l * NSJ + S_AT[j + 1]

        def wait_gated(eng, l, k):
            if k >= 6:
                eng.wait_ge(emptied_by["dve"], emptied(l * NU + UNIT_AT[("dnorm", k - 6)], "dve"))
            else:
                j = {4: 5, 5: 7, 2: 9, 3: 11, 0: 13, 1: 15}[k]
                eng.wait_ge(pv_emptied, l * NJ + j + 1)

        ctx.enter_context(nc.allow_non_contiguous_dma(reason="norm weights of a few hundred elements, turned"))
        block = ctx.enter_context(nc.Block())

        @block.sync
        def _(sp):
            def load_group(g):
                if g >= DEPTH * NG:
                    return
                l, i = divmod(g, NG)
                if g >= SLOTS:
                    wait_w_used(sp, g - SLOTS)
                if i < NGI:
                    c = 0
                    for first, n in GROUPS[i][1]:
                        sp.dma_start(w_raw[:, g % SLOTS, :, c:c + n],
                                     w_in[l, :, first:first + n].rearrange("(k p) c -> p k c", p=P)
                                     ).then_inc(w_loaded[g % SLOTS], 16)
                        c += n
                else:
                    c = (i - NGI) * GO_W
                    sp.dma_start(w_raw[:, g % SLOTS, :, 0:GO_W],
                                 w_out[l, :, c:c + GO_W].rearrange("(k p) c -> p k c", p=P)
                                 ).then_inc(w_loaded[g % SLOTS], 16)

            def spread(row, n):
                return bass.AP(tensor=row.tensor, offset=row.offset, ap=[[0, P], [1, n]])

            for tb in range(NB):
                if tb == 1:
                    sp.dma_start(gpre[:], spread(norm_pre[0:1, :], DM)).then_inc(gpre_loaded, 16)
                sp.dma_start(u_in[tb], x[0, tb * P:(tb + 1) * P, :]).then_inc(h_loaded[tb], 16)
            sp.dma_start(ident[:], ident_in).then_inc(consts_loaded, 16)
            load_group(0)
            load_group(1)
            sp.dma_start(hot[:], onehot).then_inc(consts_loaded, 16)
            sp.dma_start(heads13[0:BUCKETS, 0:12], rel_bias).then_inc(consts_loaded, 16)
            sp.dma_start(heads13[0:BUCKETS, 12:13], headrows[0:BUCKETS, 12:13]).then_inc(consts_loaded, 16)
            sp.dma_start(heads13[BUCKETS:34, :], headrows[BUCKETS:34, :]).then_inc(consts_loaded, 16)
            sp.dma_start(cc[:], rope_cc.rearrange("(t p) r -> p t r", p=P)).then_inc(consts_loaded, 16)
            sp.dma_start(ss[:], rope_ss.rearrange("(t p) r -> p t r", p=P)).then_inc(consts_loaded, 16)
            sp.dma_start(lamin[:].rearrange("p l f d -> p (l f d)"),
                         spread(diff_lambda, DEPTH * 4 * DQK)).then_inc(consts_loaded, 16)
            for half in range(2):
                sp.dma_start(subln[half * HD:(half + 1) * HD, :],
                             diff_subln.rearrange("l d -> d l")).then_inc(consts_loaded, 16)
            sp.dma_start(gq[:, :, 0], mla_q_norm[:, 0:P].rearrange("l p -> p l")).then_inc(consts_loaded, 16)
            sp.dma_start(gq[0:QL - P, :, 1], mla_q_norm[:, P:QL].rearrange("l p -> p l")).then_inc(consts_loaded, 16)
            sp.dma_start(gkv[:], mla_kv_norm.rearrange("l p -> p l")).then_inc(consts_loaded, 16)
            load_group(2)
            sp.wait_ge(table_copied, 1)
            sp.dma_start(table_dram, table[:]).then_inc(table_stored, 16)
            sp.wait_ge(table_stored, 16)

            shifts = bass.AP(tensor=table_dram.tensor, offset=table_dram.offset + P - 1,
                             ap=[[TABLE_W, 13], [-1, P], [1, SEQ]])
            sp.dma_start(strips_dram, shifts).then_inc(strips_stored, 16)
            sp.wait_ge(strips_stored, 16)

            def load_strip(dst, row):
                return sp.dma_start(dst, strips_dram[row])

            load_strip(mask[:], 12).then_inc(mask_loaded, 16)

            STRIP_ROW = {"B": 0, "C": 4, "D": 8}
            for l in range(DEPTH):
                for step in STEPS:
                    if step[0] == "unit" and step[1:] in STACKED:
                        s = STACKED.index(step[1:])
                        n = l * NU + UNIT_AT[step]
                        name, c = step[1:]
                        if s == 0 and l > 0:
                            sp.wait_ge(h_stored, 16 * NB * l)
                        wait_unit_emptied(sp, n)
                        if name == "dq" and c == 1:
                            sp.wait_ge(scores_ready, l * NS + NS_IDX)
                        parts = (0, 1, 0) if name == "dk" else (0, 0, 1)
                        for r in range(3):
                            for m in range(4):
                                if name == "qi":
                                    dst = qidx[DQK * r:DQK * (r + 1), 4 * c + m, :]
                                else:
                                    dst = dqk[c][DQK * r:DQK * (r + 1), int(name == "dk"), m, :]
                                sp.dma_start(dst.bitcast(F32), staging[DQK * m:DQK * (m + 1), s % 2, parts[r], :].bitcast(F32)
                                             ).then_inc(stack_loaded[s], 16)
                    if step == ("idx", 0):
                        for h in range(HEADS):
                            if l > 0:
                                sp.wait_ge(shifted, jobs_scored(l - 1, 8 + h))
                            load_strip(strips[:, h, :], STRIP_ROW["D"] + h).then_inc(strips_loaded[h], 16)
                    g = group_ended_by(step)
                    if g is not None:
                        load_group(l * NG + g + SLOTS)
                    if step[0] == "turn" and JOBS[step[1]][0] in "DC":
                        j = step[1]
                        h = JOBS[j][1]
                        sp.wait_ge(shifted, jobs_scored(l, j))
                        load_strip(strips[:, h, :], STRIP_ROW["CB"[j // HEADS]] + h).then_inc(strips_loaded[h], 16)
                    if step == ("turn", 7):
                        sp.wait_ge(bias_ready, (l + 1) * HEADS)
                        sp.dma_start(wuq[:, 0, :], mla_w_uq[l, 0:P, :]).then_inc(a_loaded, 16)
                        sp.dma_start(wuq[0:QL - P, 1, :], mla_w_uq[l, P:QL, :]).then_inc(a_loaded, 16)
                        sp.dma_start(wukv[:], mla_w_ukv[l]).then_inc(a_loaded, 16)
                    if step == ("turn", 12):
                        sp.wait_ge(shifted, jobs_scored(l, 11))
                        src = x[0] if l == 0 else h_dram
                        for tb in range(NB):
                            sp.dma_start(hX[:, tb, :], src[tb * P:(tb + 1) * P, :]).then_inc(h_loaded[tb], 16)
                    if step == ("turn", 15) and l + 1 < DEPTH:
                        sp.wait_ge(pv_ready, l * NJ + 15)
                        sp.dma_start(gpre[:], spread(norm_pre[l + 1:l + 2, :], DM)).then_inc(gpre_loaded, 16)
                    if step == ("out",):
                        sp.wait_ge(pv_ready, l * NJ + 16)
                        sp.dma_start(gpost[:], spread(norm_post[l:l + 1, :], DM)).then_inc(gpost_loaded, 16)
                        for c in range(NGO):
                            load_group(l * NG + NGI + c + SLOTS)
                        for tb in range(NB):
                            sp.wait_ge(h_updated, l * NB + tb + 1)
                            if l + 1 < DEPTH:
                                sp.dma_start(h_dram[tb * P:(tb + 1) * P, :], hX[:, tb, :]).then_inc(h_stored, 16)
                            else:
                                sp.dma_start(out[0, tb * P:(tb + 1) * P, :], hX[:, tb, :]).then_inc(out_stored, 16)
            sp.wait_ge(out_stored, 16 * NB)
            sp.wait_ge(h_stored, 16 * NB * (DEPTH - 1))

        @block.gpsimd
        def _(pool):
            nc.gpsimd.memset(minus_half[:], -0.5)
            nc.gpsimd.memset(ones[:], 1.0).then_inc(pool_ready, 1)

            def low(g):
                if g >= DEPTH * NG:
                    return
                pool.wait_ge(w_high_done, g + 1)
                w = WIDTH[g % NG]
                s = g % SLOTS
                nc.gpsimd.tensor_tensor(w_low[:, s, :, 0:w], w_raw[:, s, :, 0:w], w_high[:, s, :, 0:w].bitcast(F32),
                                        ALU.subtract).then_inc(w_low_done, 1)

            def root(r):
                pool.wait_ge(means_ready, r + 1)
                nc.gpsimd.tensor_tensor(roots[:, r, :], means[:, r % 2, :], minus_half[:], ALU.pow
                                        ).then_inc(roots_ready, 1)

            pool.wait_ge(pool_ready, 1)
            root(ROOT_AT[("u", 0, 0)])
            low(0)
            for tb in range(1, NB):
                root(ROOT_AT[("u", 0, tb)])
            low(1)
            for l in range(DEPTH):
                for step in STEPS:
                    g = group_ended_by(step)
                    if g is not None:
                        low(l * NG + g + 2)
                    if step[0] == "dsquares":
                        root(ROOT_AT[("d", l, step[1])])
                    if step == ("aup_head",):
                        root(ROOT_AT[("a", l, 0)])
                    if step[0] == "turn" and step[1] + 2 in (4, 5, 6, 7):
                        j = step[1] + 2
                        h = JOBS[j][1]
                        buf = probs[probs_buffers(j)[0]]
                        pool.wait_ge(select_done, l + 1)
                        pool.wait_ge(strips_loaded[h], 16 * (3 * l + 2))
                        pool.wait_ge(turn_ready, NB * (l * NJ + last_user(j) + 1))
                        for q in range(1, NB):
                            ins = nc.gpsimd.tensor_tensor(buf[:, POFF[q]:POFF[q] + WID[q]],
                                                          strips[:, h, SEQ - WID[q]:SEQ],
                                                          select[:, POFF[q] - P:POFF[q] - P + WID[q]], ALU.add)
                        ins.then_inc(bias_ready, 1)
                    if step == ("out",):
                        for c in range(NGO - 2):
                            low(l * NG + NGI + c + 2)
                        low((l + 1) * NG)
                        for tb in range(NB):
                            root(ROOT_AT[("out", l, tb)])
                            if l + 1 < DEPTH:
                                root(ROOT_AT[("u", l + 1, tb)])
                        low((l + 1) * NG + 1)

        @block.scalar
        def _(act):
            steps = [0]

            def after(ins):
                steps[0] += 1
                ins.then_inc(scalar_step, 1)
                act.wait_ge(scalar_step, steps[0])

            relus = [0]

            def high(g):
                if g >= DEPTH * NG:
                    return
                wait_w_loaded(act, g)
                w = WIDTH[g % NG]
                nc.scalar.activation(w_high[:, g % SLOTS, :, 0:w], w_raw[:, g % SLOTS, :, 0:w], ACT.Copy
                                     ).then_inc(w_high_done, 1)

            def square_h(l, tb):
                if l == 0:
                    act.wait_ge(h_loaded[tb], 16)
                else:
                    act.wait_ge(h_updated, (l - 1) * NB + tb + 1)
                src = u_in[tb] if l == 0 else hX[:, tb, :]
                after(nc.scalar.activation(waste[:], src, ACT.Square, accum_out=sumsq[:, tb:tb + 1]))
                nc.scalar.copy(sumsq[:, tb:tb + 1], sumsq[:, tb:tb + 1]).then_inc(squares_summed, 1)

            def high_u(l, tb):
                for half in range(2):
                    n = l * NU + UNIT_AT[("u", tb)] + half
                    act.wait_ge(unit_ready, n + 1)
                    nc.scalar.activation(uT[:, 0, 4 * half:4 * half + 4, tb * P:(tb + 1) * P],
                                         bank[:, WORK + n % 2, :].rearrange("p (k t) -> p k t", k=4),
                                         ACT.Copy).then_inc(high_written, 1)

            square_h(0, 0)
            high(0)
            for tb in range(NB):
                if tb + 1 < NB:
                    square_h(0, tb + 1)
                high_u(0, tb)
            high(1)
            act.wait_ge(vector_step, LAMBDA_STEPS)
            nc.scalar.activation(lamdot[:].rearrange("p l e -> p (l e)"), lamdot[:].rearrange("p l e -> p (l e)"),
                                 ACT.Exp).then_inc(lam_exp, 1)
            for l in range(DEPTH):
                for step in STEPS:
                    kind = step[0]
                    if kind == "unit":
                        name, c = step[1:]
                        n = l * NU + UNIT_AT[step]
                        b = bank[:, WORK + n % 2, :]
                        scale = {"qi": 1 / 16, "dq": DQK ** -0.5, "cqq": HD ** -0.5, "bq": HD ** -0.5}.get(name, 1.0)
                        if step[1:] in STACKED:
                            s = STACKED.index(step[1:])
                            if s >= 2:
                                act.wait_ge(stack_loaded[s - 2], 16 * STACK_DMAS * (l + 1))
                        if name in ("bv",):
                            act.wait_ge(pv_ready, l * NJ + 4)
                        if name in ("cqq", "ck"):
                            act.wait_ge(scores_ready, l * NS + NS_IDX + S_AT[2])
                        if name in ("bq", "bk"):
                            act.wait_ge(scores_ready, l * NS + NS_IDX + S_AT[4])
                        if name[0] == "g" and n > 0:
                            act.wait_ge(emptied_by["dve"], emptied(n - 1, "dve"))
                        act.wait_ge(unit_ready, n + 1)
                        if name in ("cv", "dv", "bv"):
                            v = values[1] if name == "cv" else values[0]
                            if name == "cv":
                                nc.scalar.activation(wi[:, c, :], b[:, 256:264], ACT.Copy)
                            nc.scalar.activation(v[:, c, :], b[:, 0:256], ACT.Copy).then_inc(emptied_by["act"], 1)
                        elif step[1:] == ("cq", 0):
                            nc.scalar.activation(latq[:, 0, :], b, ACT.Copy).then_inc(emptied_by["act"], 1)
                        elif step[1:] == ("cq", 1):
                            nc.scalar.activation(latq[0:96, 1, :], b[0:96, :], ACT.Copy)
                            nc.scalar.activation(kidx[64:96, :], b[96:128, :], ACT.Copy)
                            nc.scalar.activation(kidx[0:32, :], b[96:128, :], ACT.Copy).then_inc(high_written, 1)
                        elif name == "ckv":
                            nc.scalar.activation(latkv[:], b, ACT.Copy).then_inc(emptied_by["act"], 1)
                        elif name[0] == "g":
                            nc.scalar.activation(tanh[:], b, ACT.Tanh, scale=0.5).then_inc(high_written, 1)
                        else:
                            if step[1:] in STACKED:
                                dst = staging[:, STACKED.index(step[1:]) % 2, 0, :]
                            else:
                                qk = cqk if name[0] == "c" else bqk
                                dst = qk[:, int(name[1] == "k"), 0, c, :]
                            nc.scalar.activation(dst, b, ACT.Copy, scale=scale).then_inc(high_written, 1)
                    g = group_ended_by(step)
                    if g is not None:
                        high(l * NG + g + 2)
                    if kind == "idx":
                        for q in SEL_BLOCKS:
                            n = l * NS + step[1] * 3 + SEL_BLOCKS.index(q)
                            act.wait_ge(scores_ready, n + 1)
                            if relus[0] >= 4:
                                act.wait_ge(index_added, relus[0] - 3)
                            nc.scalar.activation(probs[relus[0] % 4][:, 0:WID[q]],
                                                 bank[:, SCORE + n % 3, 0:WID[q]], ACT.Relu).then_inc(relu_done, 1)
                            relus[0] += 1
                    if kind == "scores":
                        j = step[1]
                        for m in range(MAPS[j]):
                            for q in range(NB):
                                e = l * NSJ + S_AT[j] + m * NB + q
                                act.wait_ge(shifted, e + 1)
                                pr = probs[probs_buffers(j)[m]][:, POFF[q]:POFF[q] + WID[q]]
                                nc.scalar.activation(pr, pr, ACT.Exp, bias=negmax[:, j % 4, m, q:q + 1], scale=-1.0,
                                                     accum_out=sums[:, j % 4, m, q:q + 1]).then_inc(exp_done, 1)
                    if kind == "turn":
                        j = step[1]
                        jj = l * NJ + j
                        if jj >= 2:
                            act.wait_ge(pv_ready, jj - 1)
                        if j == 0 and l > 0:
                            act.wait_ge(u_ready, (l + 1) * NB)
                        for kb in range(NB):
                            t = jj * NB + kb
                            w = P * (NB - kb)
                            act.wait_ge(turn_ready, t + 1)
                            nc.scalar.activation(turned[j % 2][:, TOFF[kb]:TOFF[kb] + w],
                                                 bank[:, TURN + t % 2, 0:w], ACT.Copy).then_inc(turn_emptied, 1)
                    if kind == "aup_head":
                        act.wait_ge(scores_ready, l * NS + NS_IDX + S_AT[8])
                        wait_unit_emptied(act, l * NU + UNIT_AT[("unit", "ckv", 0)])
                        nc.scalar.activation(sq[:, 0, :], latq[:, 0, :], ACT.Square)
                        nc.scalar.activation(sq[0:64, 1, :], latq[0:64, 1, :], ACT.Square)
                        nc.scalar.activation(sq[:, 2, :], latkv[:], ACT.Square).then_inc(lat_squared, 1)
                    if kind == "aup":
                        tb = step[1]
                        n = l * NU + UNIT_AT[step]
                        r = ROOT_AT[("a", l, 0)]
                        if tb == 0:
                            act.wait_ge(roots_ready, r + 1)
                            act.wait_ge(kr_ready, l + 1)
                            act.wait_ge(pv_ready, l * NJ + 8)
                        act.wait_ge(unit_ready, n + 2)
                        kv = bank[:, WORK + (n + 1) % 2, :].rearrange("p (h t d) -> p h t d", h=HEADS, t=2)
                        if tb >= 2:
                            act.wait_ge(unit_ready, n - 4)
                        nc.scalar.activation(tokk[tb % 2][:, :, 0:HD], kv[:, :, 0, :], ACT.Copy,
                                             scale=roots[:, r, 4 + tb:5 + tb])
                        nc.scalar.activation(tokk[tb % 2][:, :, HD:A_QK],
                                             kr[:, tb, :].unsqueeze(1).to_broadcast([P, HEADS, A_ROPE]), ACT.Copy)
                        nc.scalar.activation(values[1][:, tb, :].rearrange("p (h d) -> p h d", h=HEADS),
                                             kv[:, :, 1, :], ACT.Copy,
                                             scale=roots[:, r, 4 + tb:5 + tb]).then_inc(emptied_by["act"], 1)
                        for i in range(2):
                            act.wait_ge(unit_ready, n + 3 + i)
                            nc.scalar.activation(aqk[0:A_QK, i, :, tb * P:(tb + 1) * P],
                                                 bank[0:A_QK, WORK + (n + 2 + i) % 2, :].rearrange(
                                                     "p (h t) -> p h t", h=HEADS),
                                                 ACT.Copy).then_inc(emptied_by["act"], 1)
                    if kind == "mix":
                        k = step[1]
                        wait_gated(act, l, k)
                        nc.scalar.activation(mix[:, 0, k, :], gate[:, k, :], ACT.Copy).then_inc(mix_high, 1)
                    if kind == "out":
                        for c in range(NGO - 2):
                            high(l * NG + NGI + c + 2)

                        def square_y(tb, half):
                            act.wait_ge(y_ready, (l * NGO + 2 * half + 1) * NB + tb + 1)
                            after(nc.scalar.activation(waste[:, 0:512], bank[:, 2 * tb + half, :], ACT.Square,
                                                       accum_out=ysq[:, tb, half:half + 1]))
                            nc.scalar.copy(ysq[:, tb, half:half + 1], ysq[:, tb, half:half + 1]).then_inc(y_squared, 1)

                        for tb in range(NB):
                            square_y(tb, 0)
                        high((l + 1) * NG)
                        for tb in range(NB):
                            square_y(tb, 1)
                            if l + 1 < DEPTH:
                                if tb > 0:
                                    square_h(l + 1, tb - 1)
                                if tb > 1:
                                    high_u(l + 1, tb - 2)
                        if l + 1 < DEPTH:
                            square_h(l + 1, NB - 1)
                            high_u(l + 1, NB - 2)
                            high_u(l + 1, NB - 1)
                        high((l + 1) * NG + 1)

        @block.vector
        def _(dve):
            steps = [0]

            def after(ins):
                steps[0] += 1
                ins.then_inc(vector_step, 1)
                dve.wait_ge(vector_step, steps[0])

            relus = [0]

            def mean_h(l, tb):
                r = ROOT_AT[("u", l, tb)]
                dve.wait_ge(squares_summed, l * NB + tb + 1)
                if r >= 2:
                    dve.wait_ge(roots_ready, r - 1)
                nc.vector.tensor_scalar(means[:, r % 2, 0:1], sumsq[:, tb:tb + 1], 1.0 / DM, EPS, ALU.mult, ALU.add
                                        ).then_inc(means_ready, 1)

            def norm_h(l, tb):
                r = ROOT_AT[("u", l, tb)]
                n = l * NU + UNIT_AT[("u", tb)]
                dve.wait_ge(roots_ready, r + 1)
                if tb == 0:
                    dve.wait_ge(gpre_loaded, 16 * (l + 1))
                if tb >= 2:
                    dve.wait_ge(unit_ready, n - 2)
                src = u_in[tb] if l == 0 else hX[:, tb, :]
                nc.vector.scalar_tensor_tensor(u[tb % 2][:], src, roots[:, r, 0:1], gpre[:], ALU.mult, ALU.mult
                                               ).then_inc(u_ready, 1)

            def low_u(l, tb):
                for half in range(2):
                    n = l * NU + UNIT_AT[("u", tb)] + half
                    dve.wait_ge(high_written, highs(n))
                    ks, ts = slice(4 * half, 4 * half + 4), slice(tb * P, (tb + 1) * P)
                    nc.vector.tensor_tensor(uT[:, 1, ks, ts], bank[:, WORK + n % 2, :].rearrange("p (k t) -> p k t", k=4),
                                            uT[:, 0, ks, ts].bitcast(F32), ALU.subtract).then_inc(emptied_by["dve"], 1)

            after(nc.vector.memset(means[:], 1.0))
            for tb in range(NB):
                mean_h(0, tb)
                norm_h(0, tb)
                if tb > 0:
                    low_u(0, tb - 1)
            low_u(0, NB - 1)
            dve.wait_ge(consts_loaded, 16 * N_CONSTS)
            pair = lamin[:].rearrange("p l (e t) d -> p l e t d", t=2)
            after(nc.vector.tensor_tensor(lampr[:], pair[:, :, :, 0, :], pair[:, :, :, 1, :], ALU.mult))
            after(nc.vector.tensor_reduce(lamdot[:], lampr[:], AX_X, ALU.add))
            assert steps[0] == LAMBDA_STEPS
            dve.wait_ge(table_ready, 1)
            nc.vector.tensor_copy(table[:, 0:512], bank[0:13, SCORE, :])
            nc.vector.tensor_copy(table[:, 512:TABLE_W], bank[0:13, SCORE + 1, 0:TABLE_W - 512]).then_inc(table_copied, 1)
            dve.wait_ge(lam_exp, 1)
            after(nc.vector.tensor_tensor(neglam[:], lamdot[:, :, 1], lamdot[:, :, 0], ALU.subtract))
            for l in range(DEPTH):
                after(nc.vector.tensor_scalar(neglam[:, l:l + 1], neglam[:, l:l + 1], -lam_init[l], None, ALU.add))
                after(nc.vector.tensor_scalar(subln[:, l:l + 1], subln[:, l:l + 1], 0.5 * (1.0 - lam_init[l]), None,
                                              ALU.mult))

            def select_round(r):
                q = SEL_BLOCKS[r // 16]
                row = select[:, POFF[q] - P:POFF[q] - P + WID[q]]
                after(nc.vector.max(best[:], row))
                after(nc.vector.match_replace(row, best[:], row, MARK))

            def normalise(l, j):
                dve.wait_ge(exp_done, l * NSJ + S_AT[j + 1])
                bufs = probs_buffers(j)
                i = j % 4
                if MAPS[j] == 2:
                    after(nc.vector.reciprocal(inv[:, i], sums[:, i]))
                    after(nc.vector.scalar_tensor_tensor(coef[:, i], inv[:, i, 1], neglam[:, l:l + 1], sums[:, i, 0],
                                                         ALU.mult, ALU.mult))
                    for q in range(NB):
                        sl = slice(POFF[q], POFF[q] + WID[q])
                        ins = nc.vector.scalar_tensor_tensor(probs[bufs[0]][:, sl], probs[bufs[1]][:, sl],
                                                             coef[:, i, q:q + 1], probs[bufs[0]][:, sl],
                                                             ALU.mult, ALU.add)
                else:
                    after(nc.vector.reciprocal(inv[:, i, 0], sums[:, i, 0]))
                    for q in range(NB):
                        sl = slice(POFF[q], POFF[q] + WID[q])
                        ins = nc.vector.tensor_scalar(probs[bufs[0]][:, sl], probs[bufs[0]][:, sl],
                                                      inv[:, i, 0, q:q + 1], None, ALU.mult)
                ins.then_inc(probs_ready, 1)

            for l in range(DEPTH):
                for step in STEPS:
                    kind = step[0]
                    if kind == "unit" and UNIT_READER[UNIT_AT[step]] == "dve":
                        name, c = step[1:]
                        n = l * NU + UNIT_AT[step]
                        b = bank[:, WORK + n % 2, :]
                        scale = {"qi": 1 / 16, "dq": DQK ** -0.5, "cqq": HD ** -0.5, "bq": HD ** -0.5}.get(name, 1.0)
                        dve.wait_ge(high_written, highs(n))
                        if name == "cq":
                            ins = nc.vector.tensor_tensor(kidx[32:64, :], b[96:128, :], kidx[0:32, :].bitcast(F32),
                                                          ALU.subtract)
                        elif name[0] == "g":
                            k = 2 * "abcd".index(name[1]) + c
                            ins = nc.vector.scalar_tensor_tensor(gate[:, k, :], tanh[:], 1.0, b, ALU.add, ALU.mult)
                        else:
                            if step[1:] in STACKED:
                                s = STACKED.index(step[1:])
                                hi, lo = staging[:, s % 2, 0, :], staging[:, s % 2, 1, :]
                            else:
                                qk = cqk if name[0] == "c" else bqk
                                hi, lo = (qk[:, int(name[1] == "k"), part, c, :] for part in range(2))
                            ins = nc.vector.scalar_tensor_tensor(lo, b, scale, hi.bitcast(F32), ALU.mult, ALU.subtract)
                        ins.then_inc(emptied_by["dve"], 1)
                    if kind == "idx":
                        h = step[1]
                        for q in SEL_BLOCKS:
                            row = select[:, POFF[q] - P:POFF[q] - P + WID[q]]
                            if h == 0:
                                dve.wait_ge(mask_loaded, 16)
                                wait_unit_emptied(dve, l * NU + UNIT_AT[("unit", "cv", NB - 1)])
                            before = mask[:, SEQ - WID[q]:SEQ] if h == 0 else row
                            dve.wait_ge(relu_done, relus[0] + 1)
                            if h > 0:
                                dve.wait_ge(index_added, relus[0] - 2)
                            nc.vector.scalar_tensor_tensor(row, probs[relus[0] % 4][:, 0:WID[q]], wi[:, q, h:h + 1],
                                                           before, ALU.mult, ALU.add).then_inc(index_added, 1)
                            relus[0] += 1
                    if kind == "topk":
                        if step[1] == 0:
                            dve.wait_ge(index_added, relus[0])
                        for r in range(step[1], step[2]):
                            select_round(r)
                    if kind == "selmask":
                        nc.vector.tensor_scalar(select[:], select[:], 0.5 * MARK, NEG, ALU.is_gt, ALU.mult
                                                ).then_inc(select_done, 1)
                    if kind == "scores":
                        j = step[1]
                        br, h = JOBS[j]
                        if br != "A":
                            dve.wait_ge(strips_loaded[h], 16 * (3 * l + "DCB".index(br) + 1))
                        if br == "C":
                            dve.wait_ge(bias_ready, l * HEADS + h + 1)
                        elif last_user(j) is not None:
                            dve.wait_ge(turn_ready, NB * (l * NJ + last_user(j) + 1))
                        for m in range(MAPS[j]):
                            buf = probs[probs_buffers(j)[m]]
                            for q in range(NB):
                                n = l * NS + NS_IDX + S_AT[j] + m * NB + q
                                dve.wait_ge(scores_ready, n + 1)
                                sl = buf[:, POFF[q]:POFF[q] + WID[q]]
                                bias = mask[:, SEQ - WID[q]:SEQ] if br == "A" else \
                                    sl if br == "C" and q > 0 else strips[:, h, SEQ - WID[q]:SEQ]
                                nc.vector.tensor_tensor_reduce(sl, bank[:, SCORE + n % 3, 0:WID[q]], bias, -1.0, 3.0e38,
                                                               ALU.add, ALU.min, negmax[:, j % 4, m, q:q + 1]
                                                               ).then_inc(shifted, 1)
                        if j > 0:
                            normalise(l, j - 1)
                    if step == ("turn", NJ - 1):
                        normalise(l, NJ - 1)
                    if kind == "pv":
                        j = step[1]
                        br, h = JOBS[j]
                        dve.wait_ge(pv_ready, l * NJ + j + 1)
                        if br == "D":
                            if h % 2 == 0 and (h > 0 or l > 0):
                                dve.wait_ge(unit_ready, (l if h else l - 1) * NU + UNIT_AT[("dnorm", 0 if h else 1)] + 1)
                            nc.vector.tensor_tensor(od[:, :, h % 2, :],
                                                    bank[:, PV, 0:NB * HD].rearrange("p (t d) -> p t d", d=HD),
                                                    inv[:, j % 4, 0, :].unsqueeze(2).to_broadcast([P, NB, HD]),
                                                    ALU.mult).then_inc(pv_emptied, 1)
                        else:
                            k, half = 2 * "ABC".index(br) + h // 2, h % 2
                            g = gate[HD * half:HD * (half + 1), k, :]
                            nc.vector.scalar_tensor_tensor(g, bank[0:HD, PV, :], 0.5, g, ALU.mult, ALU.mult
                                                           ).then_inc(pv_emptied, 1)
                    if kind == "dsquares":
                        r = ROOT_AT[("d", l, step[1])]
                        dve.wait_ge(pv_emptied, l * NJ + 2 * step[1] + 2)
                        after(nc.vector.tensor_tensor(odsq[:], od[:], od[:], ALU.mult))
                        after(nc.vector.tensor_reduce(dsum[:].rearrange("p (t h) -> p t h", h=2), odsq[:], AX_X, ALU.add))
                        nc.vector.tensor_scalar(means[:, r % 2, :], dsum[:], 1.0 / HD, EPS, ALU.mult, ALU.add
                                                ).then_inc(means_ready, 1)
                        dve.wait_ge(roots_ready, r + 1)
                        nc.vector.tensor_tensor(od[:], od[:],
                                                roots[:, r, :].rearrange("p (t h) -> p t h", h=2).unsqueeze(3)
                                                .to_broadcast([P, NB, 2, HD]), ALU.mult).then_inc(od_ready, 1)
                    if kind == "dnorm":
                        n = l * NU + UNIT_AT[step]
                        k = 6 + step[1]
                        dve.wait_ge(unit_ready, n + 1)
                        nc.vector.scalar_tensor_tensor(gate[:, k, :], bank[:, WORK + n % 2, :], subln[:, l:l + 1],
                                                       gate[:, k, :], ALU.mult, ALU.mult).then_inc(emptied_by["dve"], 1)
                    if kind == "aup_head":
                        n = l * NU + UNIT_AT[step]
                        r = ROOT_AT[("a", l, 0)]
                        dve.wait_ge(a_loaded, 48 * (l + 1))
                        nc.vector.tensor_scalar(wuq[:, 0, :], wuq[:, 0, :], gq[:, l, 0:1], A_QK ** -0.5, ALU.mult, ALU.mult)
                        nc.vector.tensor_scalar(wuq[0:QL - P, 1, :], wuq[0:QL - P, 1, :], gq[0:QL - P, l, 1:2],
                                                A_QK ** -0.5, ALU.mult, ALU.mult)
                        nc.vector.tensor_scalar(wukv[:], wukv[:], gkv[:, l:l + 1], None, ALU.mult).then_inc(a_folded, 1)
                        dve.wait_ge(unit_ready, n + 1)
                        s8 = bank[:, WORK + n % 2, 0:8]
                        after(nc.vector.tensor_scalar(means[:, r % 2, 0:4], s8[:, 0:4], 1.0 / QL, EPS, ALU.mult, ALU.add))
                        nc.vector.tensor_scalar(means[:, r % 2, 4:8], s8[:, 4:8], 1.0 / KVL, EPS, ALU.mult, ALU.add
                                                ).then_inc(means_ready, 1)
                        nc.vector.tensor_copy(coef[:, 0, 0:1], s8[:, 0:1]).then_inc(emptied_by["dve"], 1)
                        dve.wait_ge(unit_ready, n + 2)
                        after(nc.vector.tensor_copy(krx[:], bank[:, WORK + (n + 1) % 2, 0:NB * A_ROPE].rearrange(
                            "p (t r) -> p t r", t=NB)))
                        hr = A_ROPE // 2
                        nc.vector.tensor_tensor(kr2[:, :, 0:hr], krx[:, :, hr:], ss[:, :, 0:hr], ALU.mult)
                        nc.vector.tensor_tensor(kr2[:, :, hr:], krx[:, :, 0:hr], ss[:, :, hr:], ALU.mult)
                        after(nc.vector.tensor_tensor(kr[:], krx[:], cc[:], ALU.mult))
                        nc.vector.tensor_tensor(kr[:], kr[:], kr2[:], ALU.add).then_inc(kr_ready, 1)
                        nc.vector.tensor_copy(coef[:, 0, 0:1], krx[:, 0, 0:1]).then_inc(emptied_by["dve"], 1)
                    if kind == "aup":
                        tb = step[1]
                        n = l * NU + UNIT_AT[step]
                        r = ROOT_AT[("a", l, 0)]
                        t = tokq[tb % 2]
                        dve.wait_ge(roots_ready, r + 1)
                        dve.wait_ge(unit_ready, n + 1)
                        if tb >= 2:
                            dve.wait_ge(unit_ready, n - 5)
                        nc.vector.tensor_scalar(t[:].rearrange("p h d -> p (h d)"), bank[:, WORK + n % 2, 0:HEADS * A_QK],
                                                roots[:, r, tb:tb + 1], None, ALU.mult).then_inc(emptied_by["dve"], 1)
                        wait_unit_emptied(dve, n)
                        rot = t[:, :, HD:A_QK]
                        hr = A_ROPE // 2
                        each = lambda tab, a, b: tab[:, tb, a:b].unsqueeze(1).to_broadcast([P, HEADS, b - a])
                        nc.vector.tensor_tensor(ropet[:, :, 0:hr], rot[:, :, hr:], each(ss, 0, hr), ALU.mult)
                        after(nc.vector.tensor_tensor(ropet[:, :, hr:], rot[:, :, 0:hr], each(ss, hr, A_ROPE), ALU.mult))
                        after(nc.vector.tensor_tensor(rot, rot, each(cc, 0, A_ROPE), ALU.mult))
                        nc.vector.tensor_tensor(rot, rot, ropet[:], ALU.add).then_inc(tokq_ready, 1)
                    if kind == "mix":
                        k = step[1]
                        dve.wait_ge(mix_high, l * KC + MIX_ORDER.index(k) + 1)
                        nc.vector.tensor_tensor(mix[:, 1, k, :], gate[:, k, :], mix[:, 0, k, :].bitcast(F32),
                                                ALU.subtract).then_inc(mix_low, 1)
                    if kind == "out":
                        def scale_y(tb, half):
                            dve.wait_ge(y_squared, (2 * l + half) * NB + tb + 1)
                            nc.vector.tensor_tensor(yg[:, tb, 512 * half:512 * (half + 1)], bank[:, 2 * tb + half, :],
                                                    gpost[:, 512 * half:512 * (half + 1)], ALU.mult
                                                    ).then_inc(y_emptied, 1)

                        dve.wait_ge(gpost_loaded, 16 * (l + 1))
                        for tb in range(NB):
                            scale_y(tb, 0)
                        for tb in range(NB):
                            r = ROOT_AT[("out", l, tb)]
                            dve.wait_ge(y_squared, (2 * l + 1) * NB + tb + 1)
                            dve.wait_ge(roots_ready, r - 1)
                            after(nc.vector.tensor_tensor(dsum[:, 0:1], ysq[:, tb, 0:1], ysq[:, tb, 1:2], ALU.add))
                            nc.vector.tensor_scalar(means[:, r % 2, 0:1], dsum[:, 0:1], 1.0 / DM, EPS,
                                                    ALU.mult, ALU.add).then_inc(means_ready, 1)
                            scale_y(tb, 1)
                            dve.wait_ge(roots_ready, r + 1)
                            dve.wait_ge(y_emptied, (2 * l + 1) * NB + tb + 1)
                            dve.wait_ge(h_loaded[tb], 16 * (l + 2))
                            nc.vector.scalar_tensor_tensor(hX[:, tb, :], yg[:, tb, :], roots[:, r, 0:1], hX[:, tb, :],
                                                           ALU.mult, ALU.add).then_inc(h_updated, 1)
                            if l + 1 < DEPTH:
                                mean_h(l + 1, tb)
                                if tb > 0:
                                    low_u(l + 1, tb - 1)
                                norm_h(l + 1, tb)
                        if l + 1 < DEPTH:
                            low_u(l + 1, NB - 1)

        @block.tensor
        def _(pe):
            def work_bank(n):
                if n >= 2:
                    wait_unit_emptied(pe, n - 2)
                return bank[:, WORK + n % 2, :]

            def score_bank(l, i):
                n = l * NS + i
                if n >= 3:
                    ll, ii = divmod(n - 3, NS)
                    if ii < NS_IDX:
                        pe.wait_ge(relu_done, ll * NS_IDX + ii + 1)
                    else:
                        pe.wait_ge(shifted, ll * NSJ + ii - NS_IDX + 1)
                return bank[:, SCORE + n % 3, :]

            def turn_in(l, tb):
                n = l * NU + UNIT_AT[("u", tb)]
                pe.wait_ge(u_ready, l * NB + tb + 1)
                if l > 0 and tb == 0:
                    pe.wait_ge(y_emptied, (2 * l - 1) * NB + 1)
                for half in range(2):
                    b = work_bank(n + half)
                    for k in range(4):
                        c = (4 * half + k) * P
                        ins = nc.tensor.transpose(b[:, k * P:(k + 1) * P], u[tb % 2][:, c:c + P], ident[:])
                    ins.then_inc(unit_ready, 1)

            def three(out_ap, lh, ll, rh, rl, start, stop):
                nc.tensor.matmul(out_ap, lh, rh, start=start, stop=False)
                nc.tensor.matmul(out_ap, lh, rl, start=False, stop=False)
                return nc.tensor.matmul(out_ap, ll, rh, start=False, stop=stop)

            pe.wait_ge(consts_loaded, 16 * N_CONSTS)
            for a, b in ((0, 512), (512, TABLE_W)):
                ins = nc.tensor.matmul(bank[0:13, SCORE + a // 512, 0:b - a], heads13[:], hot[:, a:b], start=True, stop=True)
            ins.then_inc(table_ready, 1)
            for l in range(DEPTH):
                for step in STEPS:
                    kind = step[0]
                    if kind == "u":
                        turn_in(l, step[1])
                    if kind == "unit":
                        name, c = step[1:]
                        g = l * NG + GI[name]
                        s = g % SLOTS
                        n = l * NU + UNIT_AT[step]
                        token = GROUPS[GI[name]][2]
                        pe.wait_ge(w_low_done, g + 1)
                        wait_unit_emptied(pe, l * NU + UNIT_AT[("u", c if name == "cv" else NB - 1)] + 1)
                        b = work_bank(n)
                        w = WIDTH[GI[name]]
                        for k in range(KC):
                            if token:
                                ts = slice(c * P, (c + 1) * P)
                                ins = three(b[:, 0:w], uT[:, 0, k, ts], uT[:, 1, k, ts], w_high[:, s, k, 0:w],
                                            w_low[:, s, k, 0:w], k == 0, k == KC - 1)
                            else:
                                cs = slice(c * P, (c + 1) * P)
                                ins = three(b, w_high[:, s, k, cs], w_low[:, s, k, cs], uT[:, 0, k, :], uT[:, 1, k, :],
                                            k == 0, k == KC - 1)
                        ins.then_inc(unit_ready, 1)
                    if kind == "idx":
                        h = step[1]
                        if h == 0:
                            wait_unit_emptied(pe, l * NU + UNIT_AT[("unit", "cq", 1)])
                            if l == 0:
                                pe.wait_ge(table_copied, 1)
                            else:
                                pe.wait_ge(y_emptied, 2 * l * NB)
                        if h % 4 == 0:
                            pe.wait_ge(stack_loaded[h // 4], 16 * STACK_DMAS * (l + 1))
                        for i, q in enumerate(SEL_BLOCKS):
                            b = score_bank(l, h * 3 + i)
                            nc.tensor.matmul(b[:, 0:WID[q]], qidx[0:96, h, q * P:(q + 1) * P], kidx[0:96, 0:WID[q]],
                                             start=True, stop=True).then_inc(scores_ready, 1)
                    if kind == "scores":
                        j = step[1]
                        br, h = JOBS[j]
                        if br == "D" and h % 2 == 0:
                            for s in (2 + h // 2, 4 + h // 2):
                                pe.wait_ge(stack_loaded[s], 16 * STACK_DMAS * (l + 1))
                        if br in "CB" and h == 0:
                            wait_unit_emptied(pe, l * NU + UNIT_AT[("unit", "ck" if br == "C" else "bk", 1)])
                        if br == "A" and h == 0:
                            wait_unit_emptied(pe, l * NU + UNIT_AT[("aup", NB - 1)] + 3)
                        for m in range(MAPS[j]):
                            for q in range(NB):
                                b = score_bank(l, NS_IDX + S_AT[j] + m * NB + q)[:, 0:WID[q]]
                                qs, ks = slice(q * P, (q + 1) * P), slice(0, WID[q])
                                if br == "D":
                                    st = dqk[h // 2]
                                    i = 2 * (h % 2) + m
                                    ins = nc.tensor.matmul(b, st[0:96, 0, i, qs], st[0:96, 1, i, ks],
                                                           start=True, stop=True)
                                elif br == "A":
                                    ins = nc.tensor.matmul(b, aqk[0:A_QK, 0, h, qs], aqk[0:A_QK, 1, h, ks],
                                                           start=True, stop=True)
                                else:
                                    qk = cqk if br == "C" else bqk
                                    rows = slice(HD * (h % 2), HD * (h % 2) + HD)
                                    ins = three(b, qk[rows, 0, 0, h // 2, qs], qk[rows, 0, 1, h // 2, qs],
                                                qk[rows, 1, 0, h // 2, ks], qk[rows, 1, 1, h // 2, ks], True, True)
                                ins.then_inc(scores_ready, 1)
                    if kind == "turn":
                        j = step[1]
                        jj = l * NJ + j
                        pe.wait_ge(probs_ready, jj + 1)
                        if j == 0 and l > 0:
                            pe.wait_ge(y_emptied, 2 * l * NB)
                        buf = probs[probs_buffers(j)[0]]
                        for kb in range(NB):
                            t = jj * NB + kb
                            if t >= 2:
                                pe.wait_ge(turn_emptied, t - 1)
                            for q in range(kb, NB):
                                ins = nc.tensor.transpose(bank[:, TURN + t % 2, (q - kb) * P:(q - kb + 1) * P],
                                                          buf[:, POFF[q] + kb * P:POFF[q] + (kb + 1) * P], ident[:])
                            ins.then_inc(turn_ready, 1)
                    if kind == "pv":
                        j = step[1]
                        jj = l * NJ + j
                        br, h = JOBS[j]
                        v = values[0] if br in "DB" else values[1]
                        tr = turned[j % 2]
                        pe.wait_ge(turn_emptied, (jj + 1) * NB)
                        if jj > 0:
                            pe.wait_ge(pv_emptied, jj)
                        if h == 0:
                            ready = {"D": ("unit", "dv", NB - 1), "C": ("unit", "cv", NB - 1),
                                     "B": ("unit", "bv", NB - 1), "A": ("aup", NB - 1)}[br]
                            wait_unit_emptied(pe, l * NU + UNIT_AT[ready] + (3 if br == "A" else 0))
                        hs = slice(HD * h, HD * (h + 1))
                        if br == "D":
                            for q in range(NB):
                                for kb in range(q + 1):
                                    a = TOFF[kb] + (q - kb) * P
                                    ins = nc.tensor.matmul(bank[:, PV, HD * q:HD * (q + 1)], tr[:, a:a + P], v[:, kb, hs],
                                                           start=kb == 0, stop=kb == q)
                        else:
                            for kb in range(NB):
                                ins = nc.tensor.matmul(bank[0:HD, PV, kb * P:SEQ], v[:, kb, hs],
                                                       tr[:, TOFF[kb]:TOFF[kb] + P * (NB - kb)],
                                                       start=kb == 0, stop=kb == NB - 1)
                        ins.then_inc(pv_ready, 1)
                    if kind == "dnorm":
                        n = l * NU + UNIT_AT[step]
                        pe.wait_ge(od_ready, 2 * l + step[1] + 1)
                        b = work_bank(n)
                        for tb in range(NB):
                            ins = nc.tensor.transpose(b[:, tb * P:(tb + 1) * P],
                                                      od[:, tb].rearrange("p h d -> p (h d)"), ident[:])
                        ins.then_inc(unit_ready, 1)
                    if kind == "aup_head":
                        n = l * NU + UNIT_AT[step]
                        pe.wait_ge(lat_squared, l + 1)
                        b = work_bank(n)
                        for tb in range(NB):
                            ts = slice(tb * P, (tb + 1) * P)
                            nc.tensor.matmul(b[:, tb:tb + 1], sq[:, 0, ts], ones[:], start=True, stop=False)
                            nc.tensor.matmul(b[:, tb:tb + 1], sq[0:64, 1, ts], ones[0:64, :], start=False, stop=True)
                            ins = nc.tensor.matmul(b[:, 4 + tb:5 + tb], sq[:, 2, ts], ones[:], start=True, stop=True)
                        ins.then_inc(unit_ready, 1)
                        b = work_bank(n + 1)
                        for tb in range(NB):
                            ins = nc.tensor.transpose(b[:, tb * A_ROPE:(tb + 1) * A_ROPE],
                                                      latq[64:96, 1, tb * P:(tb + 1) * P], ident[64:96, 64:96])
                        ins.then_inc(unit_ready, 1)
                    if kind == "aup":
                        tb = step[1]
                        ts = slice(tb * P, (tb + 1) * P)
                        n = l * NU + UNIT_AT[step]
                        pe.wait_ge(a_folded, l + 1)
                        b = work_bank(n)[:, 0:HEADS * A_QK]
                        nc.tensor.matmul(b, latq[:, 0, ts], wuq[:, 0, :], start=True, stop=False)
                        nc.tensor.matmul(b, latq[0:64, 1, ts], wuq[0:64, 1, :], start=False, stop=True
                                         ).then_inc(unit_ready, 1)
                        b = work_bank(n + 1)
                        nc.tensor.matmul(b, latkv[:, ts], wukv[:], start=True, stop=True).then_inc(unit_ready, 1)
                        for i, tok in enumerate((tokq, tokk)):
                            if i == 0:
                                pe.wait_ge(tokq_ready, l * NB + tb + 1)
                            else:
                                wait_unit_emptied(pe, n + 1)
                            b = work_bank(n + 2 + i)
                            for h in range(HEADS):
                                ins = nc.tensor.transpose(b[0:A_QK, h * P:(h + 1) * P], tok[tb % 2][:, h, :], ident[:])
                            ins.then_inc(unit_ready, 1)
                    if kind == "out":
                        wait_unit_emptied(pe, l * NU + NU - 1)
                        wait_unit_emptied(pe, l * NU + NU - 4)
                        pe.wait_ge(turn_emptied, (l + 1) * NJ * NB)
                        pe.wait_ge(pv_emptied, (l + 1) * NJ)
                        for c in range(NGO):
                            g = l * NG + NGI + c
                            s = g % SLOTS
                            pe.wait_ge(w_low_done, g + 1)
                            for tb in range(NB):
                                ts = slice(tb * P, (tb + 1) * P)
                                b = bank[:, 2 * tb + c // 2, (c % 2) * GO_W:(c % 2 + 1) * GO_W]
                                for i, k in enumerate(MIX_ORDER):
                                    if c == 0 and tb == 0:
                                        pe.wait_ge(mix_low, l * KC + i + 1)
                                    ins = three(b, mix[:, 0, k, ts], mix[:, 1, k, ts], w_high[:, s, k, 0:GO_W],
                                                w_low[:, s, k, 0:GO_W], i == 0, i == KC - 1)
                                ins.then_inc(y_ready, 1)


_INS = ["x", "w_in", "w_out", "norm_pre", "norm_post", "mla_q_norm", "mla_kv_norm", "mla_w_uq", "mla_w_ukv",
        "diff_lambda", "diff_subln", "rel_bias"]


def bucket_of(n):
    exact = BUCKETS // 2
    nf = np.maximum(n, exact).astype(np.float32)
    large = exact + (np.log(nf / np.float32(exact)) / np.float32(np.log(2048 / exact))
                     * np.float32(BUCKETS - exact)).astype(np.int32)
    return np.where(n < exact, n, np.minimum(large, BUCKETS - 1))


def constants():
    rel = SEQ - 1 - np.arange(TABLE_W)
    onehot = np.zeros((34, TABLE_W), np.float32)
    for c, r in enumerate(rel):
        if r >= 0:
            onehot[bucket_of(np.array([r]))[0], c] = 1.0
            times = int(r <= 128) + int(r % 4 == 0) + int(r % 16 == 0)
            onehot[33, c] = np.log(times) if times else NEG
        else:
            onehot[32, c] = NEG
    headrows = np.zeros((34, 13), np.float32)
    headrows[32, :] = 1.0
    headrows[33, 0:4] = 1.0
    inv = (np.float32(10000.0) ** (-np.arange(0, A_ROPE, 2, dtype=np.float32) / np.float32(A_ROPE))).astype(np.float32)
    ang = np.arange(SEQ, dtype=np.float32)[:, None] * inv[None, :]
    cos, sin = np.cos(ang), np.sin(ang)
    return {"onehot": onehot, "headrows": headrows,
            "rope_cc": np.concatenate([cos, cos], 1).astype(np.float32),
            "rope_ss": np.concatenate([-sin, sin], 1).astype(np.float32),
            "ident": np.eye(P, dtype=np.float32)}


def kernel(**inputs):
    from concourse import bacc
    from concourse.bass_utils import run_bass_kernel_spmd

    nc = bacc.Bacc("TRN2", target_bir_lowering=False, num_devices=1)
    arrays, args = {}, []
    for name, a in [(n, inputs[n]) for n in _INS] + list(constants().items()):
        a = np.ascontiguousarray(a)
        arrays[f"in_{name}"] = a
        args.append(nc.dram_tensor(f"in_{name}", a.shape, mybir.dt.from_np(a.dtype), kind="ExternalInput").ap())
    args.append(nc.dram_tensor("out_h", (1, SEQ, DM), F32, kind="ExternalOutput").ap())
    trunk(nc, *args)
    r = run_bass_kernel_spmd(nc, [arrays], core_ids=[0])
    return r.results[0]["out_h"]
```

```python
from contextlib import ExitStack

import numpy as np

import concourse.bass as bass
from concourse import mybir

F32 = mybir.dt.float32
F32R = mybir.dt.float32r
ALU = mybir.AluOpType
ACT = mybir.ActivationFunctionType
AX_X = mybir.AxisListType.X

P = 128
DEPTH, SEQ, DM = 2, 512, 1024
NB = SEQ // P
KC = DM // P
HD = 64
HEADS = 4
A_QK, A_ROPE, QL, KVL = 96, 32, 192, 128
IDXH, DQK = 8, 32
TOPK = 128
NEG = -1e30
MARK = -3.0e38
EPS = 1e-6
BUCKETS = 32
TABLE_W = SEQ + P

OFF = {}
_at = 0
for _n, _w in (("cq", 192), ("ckv", 128), ("kr", 32), ("ga", 256), ("bq", 256), ("bk", 256), ("bv", 256),
               ("gb", 256), ("cqq", 256), ("ck", 256), ("cv", 256), ("qi", 256), ("ki", 32), ("wi", 8),
               ("gc", 256), ("dq", 256), ("dk", 256), ("dv", 256), ("gd", 256)):
    OFF[_n] = _at
    _at += _w
IN_COLS = _at

GROUPS = [
    ("cv", [(OFF["cv"], 256), (OFF["wi"], 8)], True),
    ("cq", [(OFF["cq"], 192), (OFF["kr"], 32), (OFF["ki"], 32)], False),
    ("qi", [(OFF["qi"], 256)], False),
    ("dq", [(OFF["dq"], 256)], False),
    ("dv", [(OFF["dv"], 256)], True),
    ("dk", [(OFF["dk"], 256)], False),
    ("gd", [(OFF["gd"], 256)], False),
    ("gb", [(OFF["gb"], 256)], False),
    ("ckv", [(OFF["ckv"], 128)], False),
    ("bq", [(OFF["bq"], 256)], False),
    ("bk", [(OFF["bk"], 256)], False),
    ("cqq", [(OFF["cqq"], 256)], False),
    ("ck", [(OFF["ck"], 256)], False),
    ("bv", [(OFF["bv"], 256)], True),
    ("gc", [(OFF["gc"], 256)], False),
    ("ga", [(OFF["ga"], 256)], False),
]
NGI = len(GROUPS)
NGO = 4
NG = NGI + NGO
GO_W = DM // NGO
GW = 264
GI = {g[0]: i for i, g in enumerate(GROUPS)}
WIDTH = [sum(w for _, w in g[1]) for g in GROUPS] + [GO_W] * NGO
SLOTS = 3
SEL_BLOCKS = (3, 2, 1)
N_CONSTS = 12

TOPK_ROUNDS = 3 * TOPK // 8
BRANCHES = "DBCA"
JOBS = [(b, h) for b in BRANCHES for h in range(HEADS)]
NJ = len(JOBS)
MAPS = [2 if b == "D" else 1 for b, _ in JOBS]
WID = [P * (q + 1) for q in range(NB)]
POFF = [P * q * (q + 1) // 2 for q in range(NB)]
PACK = POFF[-1] + WID[-1]
TOFF = [sum(P * (NB - k) for k in range(kb)) for kb in range(NB)]


HEAD_UNITS = [("u", 0), ("u", 1), ("unit", "cv", 0), ("u", 2), ("unit", "cv", 1), ("unit", "cv", 2), ("u", 3),
              ("unit", "cv", 3)]
FIRST_START = [("hmean", 0), ("hnorm", 0), ("hmean", 1), HEAD_UNITS[0], ("hnorm", 1), ("hmean", 2), HEAD_UNITS[1],
               HEAD_UNITS[2], ("hnorm", 2), ("hmean", 3), HEAD_UNITS[3], HEAD_UNITS[4], ("hnorm", 3), HEAD_UNITS[5],
               HEAD_UNITS[6], HEAD_UNITS[7]]
NEXT_START = [
    [0, ("hmean", 0)],
    [1, ("hnorm", 0), ("hmean", 1)],
    [2, ("hnorm", 1), ("hmean", 2), HEAD_UNITS[0], ("hnorm", 2)],
    [HEAD_UNITS[1], 3, ("hmean", 3), HEAD_UNITS[2], HEAD_UNITS[3], ("hnorm", 3), HEAD_UNITS[4], HEAD_UNITS[5],
     HEAD_UNITS[6], HEAD_UNITS[7]]
]
TOPK_START = (4, 3)
TOPK_SLOT = [(2, 0, 0, 1, 0), (0, 1, 1, 1, 1), (0, 0, 2, 1, 0), (3, 0, 2, 0, 0), (1, 0, 0, 2, 2), (1, 1, 3, 0, 2),
             (2, 1, 5, 3, 1)]
NORM_FIRST = (5, 16,)
SCORES_FIRST = (1, 2, 14, 15, 16, 17,)
TURN_LATE = (6, 7, 9, 10, 12,)
MIX_AT = {9: (6,), 11: (7,), 13: (3, 2), 14: (4,), 15: (5,), 17: (0,)}
FILL_AT = (7, 7, 7, 8)
SQUARES_AT, AUP_HEAD_AT = 8, 9


def layer_steps():
    feat = lambda g: [("unit", g, 0), ("unit", g, 1)]
    idx = lambda a, b: [("idx", h) for h in range(a, b)]
    rounds = [0]

    def topk(n):
        a = rounds[0]
        rounds[0] = min(a + n, TOPK_ROUNDS)
        return [("topk", a, rounds[0])] if rounds[0] > a else []

    st = HEAD_UNITS + feat("cq") + feat("qi")
    st += [("unit", "dq", 0)] + idx(0, 1) + [("unit", "dq", 1)] + idx(1, 2) + [("unit", "dv", 0)]
    st += idx(2, 3) + [("unit", "dv", 1)] + idx(3, 4) + [("unit", "dv", 2)] + idx(4, 5)
    st += [("unit", "dv", 3)] + idx(5, 6) + [("unit", "dk", 0)] + idx(6, 7) + idx(7, 8)
    st += topk(TOPK_START[0]) + [("unit", "dk", 1)] + topk(TOPK_START[1]) + [("unit", "gd", 0)]
    extra = {0: [("unit", "gd", 1), ("unit", "gb", 0)], 1: [("unit", "gb", 1), ("unit", "ckv", 0)],
             2: [("unit", "bq", 0), ("unit", "bq", 1)], 3: [("unit", "bk", 0), ("unit", "bk", 1)],
             4: [("unit", "cqq", 0)], 5: [("unit", "cqq", 1), ("unit", "ck", 0), ("unit", "ck", 1)],
             6: [("unit", "bv", 0), ("unit", "bv", 1), ("unit", "bv", 2), ("unit", "bv", 3), ("unit", "gc", 0)],
             7: [("unit", "gc", 1)], 8: [("unit", "ga", 0)], 9: [("unit", "ga", 1)],
             10: [("aup", 0), ("aup", 1), ("aturn", 0)],
             11: [("aup", 2), ("aturn", 1), ("aup", 3), ("aturn", 2), ("aturn", 3)]}
    late = []
    for j in range(NJ + 2):
        n = MAPS[j] * NB if j < NJ else 0
        ex = extra.get(j, [])
        r = TOPK_SLOT[j] if j < len(TOPK_SLOT) else (TOPK_ROUNDS, 0, 0, 0, 0)
        half = (len(ex) + 1) // 2
        cut = (0, 2, 5, 7, 8) if n > NB else (0, 2, 4) if ex else (0, 2, 4)
        part = [[("scores", j, a, b)] if n else [] for a, b in zip(cut, cut[1:])] + [[], []]
        norm = [("norm", j - 1)] if 0 < j <= NJ else []
        turns = [("turn", j - 1, kb) for kb in range(NB)] if norm else []
        if j == 7:
            st += topk(TOPK_ROUNDS)
        st += [("fill", 8 + i) for i, slot in enumerate(FILL_AT) if slot == j]
        st += norm + part[0] if j in NORM_FIRST else part[0] + norm
        st += late
        late = []
        if j >= NJ:
            st += [("ya", j - NJ)]
        if not ex:
            st += part[1]
        if j - 3 in (1, 3):
            st += [("dscale", (j - 3) // 2)]
        st += topk(r[0])
        for e in ex[:half]:
            st += [e] + topk(r[1])
        if ex:
            st += part[1] + turns[:2] if j in SCORES_FIRST else turns[:2] + part[1]
        if j - 3 in (1, 3):
            st += [("dnorm", (j - 3) // 2)]
        st += topk(r[2])
        for e in ex[half:]:
            st += [e] + topk(r[1])
        st += part[2]
        st += [("mix", k) for k in MIX_AT.get(j, ())]
        if j >= 2:
            st += [("pv", j - 2)]
        st += topk(r[3])
        if j == NJ:
            st += turns[:2] + [("ya", 2)] + turns[2:]
        else:
            rest = turns[2:] if ex else turns
            if j in TURN_LATE:
                rest, late = rest[:-2], rest[-2:]
            st += rest
        st += part[3]
        if j - 2 in (1, 3):
            st += [("dsquares", (j - 2) // 2)]
        st += topk(r[4])
        st += {SQUARES_AT: [("squares_a",)], AUP_HEAD_AT: [("aup_head",)]}.get(j, [])
    st += [("mix", 1)]
    assert rounds[0] == TOPK_ROUNDS
    return st


STEPS = layer_steps()


def sequence():
    seq = [(0, s) for s in FIRST_START]
    for l in range(DEPTH):
        seq += [(l, s) for s in STEPS[len(HEAD_UNITS):]] + [(l, ("y01",))]
        for tb in range(NB):
            seq += [(l, ("y", tb))]
            for s in NEXT_START[tb] if l + 1 < DEPTH else [tb]:
                seq += [(l, ("hupdate", s)) if isinstance(s, int) else (l + 1, s)]
    return seq


SEQUENCE = sequence()


def units_of(step):
    k = step[0]
    if k == "u":
        return ["dve", "dve"]
    if k == "unit":
        if step[1] in ("cv", "dv", "bv", "ckv"):
            return ["act"]
        return ["act"] if step[1:] == ("cq", 0) else ["dve"]
    if k == "dnorm":
        return ["dve"]
    if k == "aup_head":
        return ["dve", "dve"]
    if k == "aup":
        return ["dve", "act"]
    if k == "aturn":
        return ["act", "act"]
    return []


def highs_of(step):
    if step[0] == "u":
        return [True, True]
    if step[0] == "unit":
        return [units_of(step) == ["dve"]]
    return [False] * len(units_of(step))


UNIT_AT, UNIT_READER, UNIT_HIGH, UNIT_TURNED = {}, [], [], []
for _s in STEPS:
    UNIT_AT[_s] = len(UNIT_READER)
    UNIT_READER += units_of(_s)
    UNIT_HIGH += highs_of(_s)
    UNIT_TURNED += [_s[0] == "u"] * len(units_of(_s))
NU = len(UNIT_READER)


def emptied(n, who):
    full, rest = divmod(n + 1, NU)
    return full * UNIT_READER.count(who) + UNIT_READER[:rest].count(who)


def highs(n):
    full, rest = divmod(n + 1, NU)
    return full * UNIT_HIGH.count(True) + UNIT_HIGH[:rest].count(True)


ROOTS = [(l, s) for l, s in SEQUENCE if s[0] in ("hmean", "dsquares", "aup_head", "y")]
ROOT_AT = {r: i for i, r in enumerate(ROOTS)}


def y_count(l, c, tb):
    return l * NGO * NB + (c * NB + tb + 1 if c < 2 else 2 * NB + 2 * tb + c - 1)


NS_IDX = IDXH * (NB - 1)
NSJ = NB * sum(MAPS)
S_AT = [NB * sum(MAPS[:j]) for j in range(NJ + 1)]
NS = NS_IDX + NSJ
STACKED = [("qi", 0), ("qi", 1), ("dq", 0), ("dq", 1), ("dk", 0), ("dk", 1)]
STACK_DMAS = 3
STACK_AT = {("unit", "qi", 1): 0, ("unit", "dq", 0): 1, ("unit", "dq", 1): 2, ("unit", "dv", 3): 3,
            ("unit", "dk", 1): 4, ("unit", "gd", 0): 5}
MIX_ORDER = [6, 7, 2, 3, 4, 5, 0, 1]
EARLY = 4


def probs_buffers(j):
    return [2 * (j % 2), 2 * (j % 2) + 1] if JOBS[j][0] == "D" else [j % 4]


def last_user(j):
    mine = set(probs_buffers(j))
    for i in range(j - 1, -1, -1):
        if mine & set(probs_buffers(i)):
            return i
    return None


def group_ended_by(step):
    if step[0] != "unit":
        return None
    _, cols, token = GROUPS[GI[step[1]]]
    last = NB - 1 if token else (sum(w for _, w in cols) + P - 1) // P - 1
    return GI[step[1]] if step[2] == last else None


CONVERT_AFTER = {3: 3, 5: 5}


def convert_steps():
    at = {("unit", "cv", 1): [1], ("unit", "cv", 3): [2], ("y01",): [NGI + 3], ("y", 0): [NG]}
    for g in range(3, NGI + 3):
        freed = next(i for i, s in enumerate(STEPS) if group_ended_by(s) == g - SLOTS)
        cost = 0
        for s in STEPS[freed + 1:]:
            cost += {"unit": 1 if s[0] == "unit" and GROUPS[GI[s[1]]][2] else 2, "aup": 1, "pv": 1}.get(s[0], 0)
            if cost >= CONVERT_AFTER.get(g, 4):
                break
        at.setdefault(s, []).append(g)
    return at


CONVERT_AT = convert_steps()


LAST_UNIT = [UNIT_AT[s] for g in range(NGI) for s in STEPS if group_ended_by(s) == g]
def trunk(nc, x, w_in, w_out, norm_pre, norm_post, mla_q_norm, mla_kv_norm, mla_w_uq, mla_w_ukv,
          diff_lambda, diff_subln, rel_bias, onehot, headrows, rope_cc, rope_ss, ident_in, out):
    lam_init = [0.8 - 0.6 * float(np.exp(-0.3 * l)) for l in range(DEPTH)]
    h_dram = nc.dram_tensor("h_dram", [SEQ, DM], F32, kind="Internal").ap()
    parts_dram = nc.dram_tensor("parts_dram", [2, P, 2, SEQ], F32, kind="Internal").ap()
    strips_dram = nc.dram_tensor("strips_dram", [13, P, SEQ], F32, kind="Internal").ap()
    table_dram = nc.dram_tensor("table_dram", [13, TABLE_W], F32, kind="Internal").ap()

    with ExitStack() as ctx:
        base = (nc.sbuf_base + 63) // 64 * 64
        top = [base]
        arena = {}

        def room(name, nbytes):
            arena[name] = top[0]
            top[0] += (nbytes + 31) // 32 * 32
            assert top[0] <= nc.sbuf_usable_end, (name, top[0] - nc.sbuf_usable_end)

        def at(name, room_name, shape, dt, skip=0):
            return nc.alloc_sbuf_tensor_at(name, shape, dt, offset=arena[room_name] + skip)

        KB = 1024
        room("raw", SLOTS * KC * GW * 4)
        room("high", SLOTS * KC * GW * 4)
        room("uT", 32 * KB)
        room("gate", 16 * KB)
        for i in range(4):
            room(f"probs{i}", PACK * 4)
        for i in range(2):
            room(f"turned{i}", PACK * 4)
        room("values0", 4 * KB)
        room("values1", 4 * KB)
        room("X", 16 * KB)
        room("Y", 16 * KB)
        room("staging", 8 * KB)
        room("select", (PACK - P) * 4)
        room("kidx", 2 * KB)
        room("strips", 8 * KB)
        room("mask", 2 * KB)
        room("latent", 6 * KB)
        room("wukv", 2 * KB)
        room("wuq", 3 * KB)
        room("small", 4 * KB)
        w_raw = at("w_raw", "raw", [P, SLOTS, KC, GW], F32)
        w_low = at("w_low", "raw", [P, SLOTS, KC, GW], F32R)
        w_high = at("w_high", "high", [P, SLOTS, KC, GW], F32R)
        uT = at("uT", "uT", [P, 2, KC, SEQ], F32R)
        mix = at("mix", "uT", [P, 2, KC, SEQ], F32R)
        gate = at("gate", "gate", [P, KC, SEQ], F32)
        probs = [at(f"probs{i}", f"probs{i}", [P, PACK], F32) for i in range(4)]
        turned = [at(f"turned{i}", f"turned{i}", [P, PACK], F32) for i in range(2)]
        values = [at(f"values{i}", f"values{i}", [P, NB, HEADS * HD], F32) for i in range(2)]
        hX = at("hX", "X", [P, NB, DM], F32)
        qidx = at("qidx", "X", [P, IDXH, SEQ], F32R)
        dqk = [at(f"dqk{c}", "YX"[c], [P, 2, 4, SEQ], F32R) for c in range(2)]
        cqk = at("cqk", "X", [P, 2, 2, 2, SEQ], F32R)
        bqk = at("bqk", "Y", [P, 2, 2, 2, SEQ], F32R)
        aqk = at("aqk", "Y", [P, 2, HEADS, SEQ], F32)
        yg = at("yg", "Y", [P, NB, DM], F32)
        staging = at("staging", "staging", [P, 2, 2, SEQ], F32R)
        tokq = [at(f"tokq{i}", "staging", [P, HEADS, A_QK], F32, skip=1536 * i) for i in range(2)]
        tokk = [at(f"tokk{i}", "staging", [P, HEADS, A_QK], F32, skip=3072 + 1536 * i) for i in range(2)]
        ropet = at("ropet", "staging", [P, HEADS, A_ROPE], F32, skip=6144)
        kr = at("kr", "staging", [P, NB, A_ROPE], F32, skip=6656)
        kr2 = at("kr2", "staging", [P, NB, A_ROPE], F32, skip=7168)
        krx = at("krx", "staging", [P, NB, A_ROPE], F32, skip=7680)
        odsq = at("odsq", "staging", [P, NB, 2, HD], F32)
        sq = at("sq", "staging", [P, 3, SEQ], F32)
        od = at("od", "staging", [P, NB, 2, HD], F32, skip=2 * KB)
        select = at("select", "select", [P, PACK - P], F32)
        kidx = at("kidx", "kidx", [P, SEQ], F32R)
        strips = at("strips", "strips", [P, HEADS, SEQ], F32)
        mask = at("mask", "mask", [P, SEQ], F32)
        latq = at("latq", "latent", [P, 2, SEQ], F32)
        wuq = at("wuq", "wuq", [P, 2, HEADS * A_QK], F32)
        wukv = at("wukv", "wukv", [P, HEADS * P], F32)
        latkv = at("latkv", "latent", [P, SEQ], F32, skip=4 * KB)
        u = [at(f"u{i}", f"probs{i}", [P, DM], F32) for i in range(2)]
        waste = at("waste", "probs2", [P, DM], F32)
        gpre = at("gpre", "turned0", [P, DM], F32)
        gpost = at("gpost", "turned1", [P, DM], F32)
        hot = at("hot", "Y", [34, TABLE_W], F32)
        heads13 = at("heads13", "Y", [34, 13], F32, skip=3 * KB)
        table = at("table", "Y", [13, TABLE_W], F32, skip=4 * KB)
        lamin = at("lamin", "Y", [P, DEPTH, 4, DQK], F32, skip=8 * KB)
        lampr = at("lampr", "Y", [P, DEPTH, 2, DQK], F32, skip=10 * KB)
        tiny_at = [arena["small"]]

        def tiny(name, shape):
            n = (4 * int(np.prod(shape[1:])) + 31) // 32 * 32
            t = nc.alloc_sbuf_tensor_at(name, shape, F32, offset=tiny_at[0])
            tiny_at[0] += n
            assert tiny_at[0] <= top[0]
            return t

        ident = tiny("ident", [P, P])
        cc = tiny("cc", [P, NB, A_ROPE])
        ss = tiny("ss", [P, NB, A_ROPE])
        wi = tiny("wi", [P, NB, IDXH])
        best = tiny("best", [P, 8])
        negmax = tiny("negmax", [P, 4, 2, NB])
        sums = tiny("sums", [P, 4, 2, NB])
        inv = tiny("inv", [P, 4, 2, NB])
        coef = tiny("coef", [P, 4, NB])
        sumsq = tiny("sumsq", [P, NB])
        ysq = tiny("ysq", [P, NB, 2])
        dsum = tiny("dsum", [P, 2 * NB])
        means = tiny("means", [P, 2, 8])
        roots = tiny("roots", [P, len(ROOTS), 8])
        minus_half = tiny("minus_half", [P, 8])
        ones = tiny("ones", [P, 1])
        lamdot = tiny("lamdot", [P, DEPTH, 2])
        neglam = tiny("neglam", [P, DEPTH])
        subln = tiny("subln", [P, DEPTH])
        gq = tiny("gq", [P, DEPTH, 2])
        gkv = tiny("gkv", [P, DEPTH])

        bank = ctx.enter_context(nc.psum_tensor("bank", [P, 8, 512], F32))
        WORK, SCORE, TURN, PV = 0, 2, 5, 7

        def unit_bank(n):
            l, i = divmod(n, NU)
            if UNIT_TURNED[i]:
                return SCORE + i % 2
            return WORK + (l * (NU - sum(UNIT_TURNED)) + i - sum(UNIT_TURNED[:i])) % 2

        def sem(name):
            return ctx.enter_context(nc.semaphore(name))

        consts_loaded, ident_loaded = sem("consts_loaded"), sem("ident_loaded")
        lam_dots = sem("lam_dots")
        table_ready, table_copied, table_stored = sem("table_ready"), sem("table_copied"), sem("table_stored")
        pool_ready, strips_stored = sem("pool_ready"), sem("strips_stored")
        strips_loaded = [sem(f"strips_loaded{h}") for h in range(HEADS)]
        mask_loaded = sem("mask_loaded")
        h_loaded = [sem(f"h_loaded{t}") for t in range(NB)]
        h_updated, h_stored = sem("h_updated"), sem("h_stored")
        gpre_loaded, gpost_loaded, a_loaded = sem("gpre_loaded"), sem("gpost_loaded"), sem("a_loaded")
        w_loaded = [sem(f"w_loaded{i}") for i in range(SLOTS)]
        w_high_done, w_low_done = sem("w_high_done"), sem("w_low_done")
        squares_summed, means_ready, roots_ready = sem("squares_summed"), sem("means_ready"), sem("roots_ready")
        u_ready = sem("u_ready")
        unit_ready, high_written = sem("unit_ready"), sem("high_written")
        emptied_by = {"act": sem("emptied_by_act"), "dve": sem("emptied_by_dve")}
        parts_stored = [sem(f"parts_stored{i}") for i in range(2)]
        stack_loaded = [sem(f"stack_loaded{i}") for i in range(len(STACKED))]
        scores_ready, relu_done, index_added = sem("scores_ready"), sem("relu_done"), sem("index_added")
        select_done, bias_ready = sem("select_done"), sem("bias_ready")
        shifted, exp_done, probs_ready = sem("shifted"), sem("exp_done"), sem("probs_ready")
        turn_ready, turn_emptied = sem("turn_ready"), sem("turn_emptied")
        pv_ready, pv_emptied = sem("pv_ready"), sem("pv_emptied")
        od_ready, a_folded, lat_squared = sem("od_ready"), sem("a_folded"), sem("lat_squared")
        tokq_ready, kr_ready = sem("tokq_ready"), sem("kr_ready")
        mix_high, mix_low = sem("mix_high"), sem("mix_low")
        y_ready, y_squared, y_emptied = sem("y_ready"), sem("y_squared"), sem("y_emptied")
        vector_step, lam_exp = sem("vector_step"), sem("lam_exp")
        out_stored = sem("out_stored")

        def wait_unit_emptied(eng, n):
            who = UNIT_READER[n % NU]
            eng.wait_ge(emptied_by[who], emptied(n, who))

        def wait_w_loaded(eng, g):
            eng.wait_ge(w_loaded[g % SLOTS], 16 * sum(len(GROUPS[i % NG][1]) if i % NG < NGI else 1
                                                      for i in range(g % SLOTS, g + 1, SLOTS)))

        def wait_w_used(eng, g):
            l, i = divmod(g, NG)
            if i < NGI:
                eng.wait_ge(unit_ready, l * NU + LAST_UNIT[i] + 1)
            else:
                eng.wait_ge(y_ready, y_count(l, i - NGI, NB - 1))

        def jobs_scored(l, j):
            return l * NSJ + S_AT[j + 1]

        def wait_gated(eng, l, k):
            if k >= 6:
                eng.wait_ge(emptied_by["dve"], emptied(l * NU + UNIT_AT[("dnorm", k - 6)], "dve"))
            else:
                j = {2: 5, 3: 7, 4: 9, 5: 11, 0: 13, 1: 15}[k]
                eng.wait_ge(pv_emptied, l * NJ + j + 1)

        ctx.enter_context(nc.allow_non_contiguous_dma(reason="norm weights of a few hundred elements, turned"))
        block = ctx.enter_context(nc.Block())

        @block.sync
        def _(sp):
            def load_group(g):
                if g >= DEPTH * NG:
                    return
                l, i = divmod(g, NG)
                if g >= SLOTS:
                    wait_w_used(sp, g - SLOTS)
                if i < NGI:
                    c = 0
                    for first, n in GROUPS[i][1]:
                        sp.dma_start(w_raw[:, g % SLOTS, :, c:c + n],
                                     w_in[l, :, first:first + n].rearrange("(k p) c -> p k c", p=P)
                                     ).then_inc(w_loaded[g % SLOTS], 16)
                        c += n
                else:
                    c = (i - NGI) * GO_W
                    sp.dma_start(w_raw[:, g % SLOTS, :, 0:GO_W],
                                 w_out[l, :, c:c + GO_W].rearrange("(k p) c -> p k c", p=P)
                                 ).then_inc(w_loaded[g % SLOTS], 16)

            def spread(row, n):
                return bass.AP(tensor=row.tensor, offset=row.offset, ap=[[0, P], [1, n]])

            for tb in range(NB):
                sp.dma_start(hX[:, tb, :], x[0, tb * P:(tb + 1) * P, :]).then_inc(h_loaded[tb], 16)
                if tb == 0:
                    sp.dma_start(gpre[:], spread(norm_pre[0:1, :], DM)).then_inc(gpre_loaded, 16)
                    sp.dma_start(ident[:], ident_in).then_inc(ident_loaded, 16)
                if tb == 1:
                    load_group(0)
            load_group(1)
            sp.dma_start(hot[:], onehot).then_inc(consts_loaded, 16)
            sp.dma_start(heads13[0:BUCKETS, 0:12], rel_bias).then_inc(consts_loaded, 16)
            sp.dma_start(heads13[0:BUCKETS, 12:13], headrows[0:BUCKETS, 12:13]).then_inc(consts_loaded, 16)
            sp.dma_start(heads13[BUCKETS:34, :], headrows[BUCKETS:34, :]).then_inc(consts_loaded, 16)
            sp.dma_start(cc[:], rope_cc.rearrange("(t p) r -> p t r", p=P)).then_inc(consts_loaded, 16)
            sp.dma_start(ss[:], rope_ss.rearrange("(t p) r -> p t r", p=P)).then_inc(consts_loaded, 16)
            sp.dma_start(lamin[:].rearrange("p l f d -> p (l f d)"),
                         spread(diff_lambda, DEPTH * 4 * DQK)).then_inc(consts_loaded, 16)
            for half in range(2):
                sp.dma_start(subln[half * HD:(half + 1) * HD, :],
                             diff_subln.rearrange("l d -> d l")).then_inc(consts_loaded, 16)
            sp.dma_start(gq[:, :, 0], mla_q_norm[:, 0:P].rearrange("l p -> p l")).then_inc(consts_loaded, 16)
            sp.dma_start(gq[0:QL - P, :, 1], mla_q_norm[:, P:QL].rearrange("l p -> p l")).then_inc(consts_loaded, 16)
            sp.dma_start(gkv[:], mla_kv_norm.rearrange("l p -> p l")).then_inc(consts_loaded, 16)
            load_group(2)
            STRIP_ROW = {"B": 0, "C": 4, "D": 8}

            def load_strip(dst, row):
                return sp.dma_start(dst, strips_dram[row])

            for l, step in SEQUENCE:
                if (l, step) == (0, ("unit", "cq", 1)):
                    sp.wait_ge(table_copied, 1)
                    sp.dma_start(table_dram, table[:]).then_inc(table_stored, 16)
                    sp.wait_ge(table_stored, 16)
                    shifts = bass.AP(tensor=table_dram.tensor, offset=table_dram.offset + P - 1,
                                     ap=[[TABLE_W, 13], [-1, P], [1, SEQ]])
                    sp.dma_start(strips_dram, shifts).then_inc(strips_stored, 16)
                    sp.wait_ge(strips_stored, 16)
                    load_strip(mask[:], 12).then_inc(mask_loaded, 16)
                if step in STACK_AT:
                    s = STACK_AT[step]
                    name, c = STACKED[s]
                    if s == 0 and l > 0:
                        sp.wait_ge(h_stored, 16 * NB * l)
                    if c == 1 and name != "qi":
                        sp.wait_ge(scores_ready, l * NS + NS_IDX // (2 if name == "dq" else 1))
                    sp.wait_ge(parts_stored[s % 2], 16 * (3 * l + s // 2 + 1))
                    for r, part in enumerate((0, 1, 0) if name == "dk" else (0, 0, 1)):
                        rows = slice(DQK * r, DQK * (r + 1))
                        dst = qidx[rows, 4 * c:4 * c + 4, :] if name == "qi" else dqk[c][rows, int(name == "dk"), :, :]
                        src = parts_dram[s % 2, :, part, :].rearrange("(m p) t -> p m t", p=DQK)
                        sp.dma_start(dst.bitcast(F32), src).then_inc(stack_loaded[s], 16)
                g = group_ended_by(step)
                if g is not None:
                    load_group(l * NG + g + SLOTS)
                if step[0] == "unit" and step[1:] in STACKED:
                    s = STACKED.index(step[1:])
                    wait_unit_emptied(sp, l * NU + UNIT_AT[step])
                    before = 6 * l + s - 2
                    if before >= 0:
                        sp.wait_ge(stack_loaded[before % 6], 16 * STACK_DMAS * (before // 6 + 1))
                    sp.dma_start(parts_dram[s % 2], staging[:, s % 2].bitcast(F32)).then_inc(parts_stored[s % 2], 16)
                if step == ("idx", 0):
                    for h in range(HEADS):
                        if l > 0:
                            sp.wait_ge(shifted, jobs_scored(l - 1, 8 + h))
                        load_strip(strips[:, h, :], STRIP_ROW["D"] + h).then_inc(strips_loaded[h], 16)
                if step[0] == "norm" and JOBS[step[1]][0] in "DB":
                    j = step[1]
                    h = JOBS[j][1]
                    sp.wait_ge(shifted, jobs_scored(l, j))
                    load_strip(strips[:, h, :], STRIP_ROW[BRANCHES[j // HEADS + 1]] + h
                               ).then_inc(strips_loaded[h], 16)
                if step == ("norm", 3):
                    sp.dma_start(wuq[:, 0, :], mla_w_uq[l, 0:P, :]).then_inc(a_loaded, 16)
                    sp.dma_start(wuq[0:QL - P, 1, :], mla_w_uq[l, P:QL, :]).then_inc(a_loaded, 16)
                    sp.dma_start(wukv[:], mla_w_ukv[l]).then_inc(a_loaded, 16)
                if step == ("norm", 12):
                    sp.wait_ge(shifted, jobs_scored(l, 11))
                    src = x[0] if l == 0 else h_dram
                    for tb in range(NB):
                        sp.dma_start(hX[:, tb, :], src[tb * P:(tb + 1) * P, :]).then_inc(h_loaded[tb], 16)
                if step == ("norm", 15) and l + 1 < DEPTH:
                    sp.wait_ge(pv_ready, l * NJ + 15)
                    sp.dma_start(gpre[:], spread(norm_pre[l + 1:l + 2, :], DM)).then_inc(gpre_loaded, 16)
                if step == ("y01",):
                    sp.wait_ge(pv_ready, l * NJ + 16)
                    sp.dma_start(gpost[:], spread(norm_post[l:l + 1, :], DM)).then_inc(gpost_loaded, 16)
                    for c in range(2):
                        load_group(l * NG + NGI + c + SLOTS)
                if step[0] == "hupdate":
                    tb = step[1]
                    if tb == NB - 1:
                        for c in range(2, NGO):
                            load_group(l * NG + NGI + c + SLOTS)
                    sp.wait_ge(h_updated, l * NB + tb + 1)
                    if l + 1 < DEPTH:
                        sp.dma_start(h_dram[tb * P:(tb + 1) * P, :], hX[:, tb, :]).then_inc(h_stored, 16)
                    else:
                        sp.dma_start(out[0, tb * P:(tb + 1) * P, :], hX[:, tb, :]).then_inc(out_stored, 16)
            sp.wait_ge(out_stored, 16 * NB)
            sp.wait_ge(h_stored, 16 * NB * (DEPTH - 1))

        @block.gpsimd
        def _(pool):
            nc.gpsimd.memset(minus_half[:], -0.5)
            nc.gpsimd.memset(ones[:], 1.0).then_inc(pool_ready, 1)

            def low(g):
                if g >= DEPTH * NG:
                    return
                if g == 1:
                    pool.wait_ge(w_low_done, 1)
                pool.wait_ge(w_high_done, g + 1)
                w = WIDTH[g % NG]
                s = g % SLOTS
                nc.gpsimd.tensor_tensor(w_low[:, s, :, 0:w], w_raw[:, s, :, 0:w], w_high[:, s, :, 0:w].bitcast(F32),
                                        ALU.subtract).then_inc(w_low_done, 1)

            def root(r):
                pool.wait_ge(means_ready, r + 1)
                n = 1 if ROOTS[r][1][0] in ("y", "hmean") else 8
                nc.gpsimd.tensor_tensor(roots[:, r, 0:n], means[:, r % 2, 0:n], minus_half[:, 0:n], ALU.pow
                                        ).then_inc(roots_ready, 1)

            pool.wait_ge(pool_ready, 1)
            for l, step in SEQUENCE:
                if (l, step) in ROOT_AT:
                    root(ROOT_AT[l, step])
                for g in CONVERT_AT.get(step, ()):
                    low(l * NG + g)
                if step[0] == "fill":
                    j = step[1]
                    h = JOBS[j][1]
                    buf = probs[probs_buffers(j)[0]]
                    pool.wait_ge(select_done, l + 1)
                    pool.wait_ge(strips_loaded[h], 16 * (3 * l + 3))
                    pool.wait_ge(turn_ready, NB * (l * NJ + last_user(j) + 1))
                    for q in range(1, NB):
                        ins = nc.gpsimd.tensor_tensor(buf[:, POFF[q]:POFF[q] + WID[q]],
                                                      strips[:, h, SEQ - WID[q]:SEQ],
                                                      select[:, POFF[q] - P:POFF[q] - P + WID[q]], ALU.add)
                    ins.then_inc(bias_ready, 1)

        @block.scalar
        def _(act):
            relus = [0]

            def high(g):
                if g >= DEPTH * NG:
                    return
                wait_w_loaded(act, g)
                w = WIDTH[g % NG]
                nc.scalar.activation(w_high[:, g % SLOTS, :, 0:w], w_raw[:, g % SLOTS, :, 0:w], ACT.Copy
                                     ).then_inc(w_high_done, 1)

            squared = {squares_summed: 0, y_squared: 0}

            def waste_free(done):
                for what, n in squared.items():
                    if n:
                        act.wait_ge(what, n)
                squared[done] += 1

            def square_h(l, tb):
                waste_free(squares_summed)
                if l == 0:
                    act.wait_ge(h_loaded[tb], 16)
                else:
                    act.wait_ge(h_updated, (l - 1) * NB + tb + 1)
                nc.scalar.activation(waste[:], hX[:, tb, :], ACT.Square, accum_out=sumsq[:, tb:tb + 1]
                                     ).then_inc(squares_summed, 1)

            def square_y(l, tb, half):
                waste_free(y_squared)
                act.wait_ge(y_ready, y_count(l, 2 * half + 1, tb))
                nc.scalar.activation(waste[:, 0:512], bank[:, 2 * tb + half, :], ACT.Square,
                                     accum_out=ysq[:, tb, half:half + 1]).then_inc(y_squared, 1)

            def high_u(l, tb):
                for half in range(2):
                    n = l * NU + UNIT_AT[("u", tb)] + half
                    act.wait_ge(unit_ready, n + 1)
                    nc.scalar.activation(uT[:, 0, 4 * half:4 * half + 4, tb * P:(tb + 1) * P],
                                         bank[:, unit_bank(n), :].rearrange("p (k t) -> p k t", k=4),
                                         ACT.Copy).then_inc(high_written, 1)

            for l, step in SEQUENCE:
                kind = step[0]
                if kind == "hmean":
                    square_h(l, step[1])
                if kind == "u":
                    high_u(l, step[1])
                if (l, step) == (0, ("u", 0)):
                    high(0)
                if (l, step) == (0, ("unit", "qi", 0)):
                    act.wait_ge(lam_dots, 1)
                    nc.scalar.activation(lamdot[:].rearrange("p l e -> p (l e)"),
                                         lamdot[:].rearrange("p l e -> p (l e)"), ACT.Exp).then_inc(lam_exp, 1)
                if kind == "unit":
                    name, c = step[1:]
                    n = l * NU + UNIT_AT[step]
                    b = bank[:, unit_bank(n), :]
                    scale = {"qi": 1 / 16, "dq": DQK ** -0.5, "cqq": HD ** -0.5, "bq": HD ** -0.5}.get(name, 1.0)
                    if step[1:] in STACKED:
                        s = STACKED.index(step[1:])
                        if s >= 2:
                            act.wait_ge(parts_stored[s % 2], 16 * (3 * l + s // 2))
                    if name in ("bv",):
                        act.wait_ge(pv_ready, l * NJ + 4)
                    if name in ("bq", "bk"):
                        act.wait_ge(scores_ready, l * NS + NS_IDX + S_AT[2])
                    if name in ("cqq", "ck"):
                        act.wait_ge(scores_ready, l * NS + NS_IDX + S_AT[4])
                    act.wait_ge(unit_ready, n + 1)
                    if name in ("cv", "dv", "bv"):
                        v = values[1] if name == "cv" else values[0]
                        if name == "cv":
                            nc.scalar.activation(wi[:, c, :], b[:, 256:264], ACT.Copy)
                        nc.scalar.activation(v[:, c, :], b[:, 0:256], ACT.Copy).then_inc(emptied_by["act"], 1)
                    elif step[1:] == ("cq", 0):
                        nc.scalar.activation(latq[:, 0, :], b, ACT.Copy).then_inc(emptied_by["act"], 1)
                    elif step[1:] == ("cq", 1):
                        nc.scalar.activation(latq[0:96, 1, :], b[0:96, :], ACT.Copy)
                        nc.scalar.activation(kidx[64:96, :], b[96:128, :], ACT.Copy)
                        nc.scalar.activation(kidx[0:32, :], b[96:128, :], ACT.Copy).then_inc(high_written, 1)
                    elif name == "ckv":
                        nc.scalar.activation(latkv[:], b, ACT.Copy).then_inc(emptied_by["act"], 1)
                    elif name[0] == "g":
                        k = 2 * "abcd".index(name[1]) + c
                        nc.scalar.activation(gate[:, k, :], b, ACT.Tanh, scale=0.5).then_inc(high_written, 1)
                    else:
                        if step[1:] in STACKED:
                            dst = staging[:, STACKED.index(step[1:]) % 2, 0, :]
                        else:
                            qk = cqk if name[0] == "c" else bqk
                            dst = qk[:, int(name[1] == "k"), 0, c, :]
                        nc.scalar.activation(dst, b, ACT.Copy, scale=scale).then_inc(high_written, 1)
                if kind not in ("y01", "y"):
                    for g in CONVERT_AT.get(step, ()):
                        high(l * NG + g)
                if kind == "idx":
                    for q in SEL_BLOCKS:
                        n = l * NS + step[1] * 3 + SEL_BLOCKS.index(q)
                        act.wait_ge(scores_ready, n + 1)
                        if relus[0] >= 4:
                            act.wait_ge(index_added, relus[0] - 3)
                        nc.scalar.activation(probs[relus[0] % 4][:, 0:WID[q]],
                                             bank[:, SCORE + n % 3, 0:WID[q]], ACT.Relu).then_inc(relu_done, 1)
                        relus[0] += 1
                if kind == "scores":
                    j = step[1]
                    for i in range(step[2], step[3]):
                        m, q = divmod(i, NB)
                        act.wait_ge(shifted, l * NSJ + S_AT[j] + i + 1)
                        pr = probs[probs_buffers(j)[m]][:, POFF[q]:POFF[q] + WID[q]]
                        nc.scalar.activation(pr, pr, ACT.Exp, bias=negmax[:, j % 4, m, q:q + 1], scale=-1.0,
                                             accum_out=sums[:, j % 4, m, q:q + 1]).then_inc(exp_done, 1)
                if kind == "turn":
                    j, kb = step[1:]
                    jj = l * NJ + j
                    if kb == 0 and jj >= 2:
                        act.wait_ge(pv_ready, jj - 1)
                    if kb == 0 and j == 0 and l > 0:
                        act.wait_ge(u_ready, (l + 1) * NB)
                    t = jj * NB + kb
                    w = P * (NB - kb)
                    act.wait_ge(turn_ready, t + 1)
                    nc.scalar.activation(turned[j % 2][:, TOFF[kb]:TOFF[kb] + w], bank[:, TURN + t % 2, 0:w],
                                         ACT.Copy).then_inc(turn_emptied, 1)
                if kind == "squares_a":
                    act.wait_ge(emptied_by["dve"], emptied(l * NU + UNIT_AT[("dnorm", 1)], "dve"))
                    wait_unit_emptied(act, l * NU + UNIT_AT[("unit", "ckv", 0)])
                    nc.scalar.activation(sq[:, 0, :], latq[:, 0, :], ACT.Square)
                    nc.scalar.activation(sq[0:64, 1, :], latq[0:64, 1, :], ACT.Square)
                    nc.scalar.activation(sq[:, 2, :], latkv[:], ACT.Square).then_inc(lat_squared, 1)
                if kind == "aup":
                    tb = step[1]
                    n = l * NU + UNIT_AT[step]
                    r = ROOT_AT[l, ("aup_head",)]
                    if tb == 0:
                        act.wait_ge(roots_ready, r + 1)
                        act.wait_ge(kr_ready, l + 1)
                        act.wait_ge(pv_ready, l * NJ + 8)
                    act.wait_ge(unit_ready, n + 2)
                    kv = bank[:, unit_bank(n + 1), :].rearrange("p (h t d) -> p h t d", h=HEADS, t=2)
                    if tb >= 2:
                        act.wait_ge(unit_ready, l * NU + UNIT_AT[("aturn", tb - 2)] + 2)
                    nc.scalar.activation(tokk[tb % 2][:, :, 0:HD], kv[:, :, 0, :], ACT.Copy,
                                         scale=roots[:, r, 4 + tb:5 + tb])
                    nc.scalar.activation(tokk[tb % 2][:, :, HD:A_QK],
                                         kr[:, tb, :].unsqueeze(1).to_broadcast([P, HEADS, A_ROPE]), ACT.Copy)
                    nc.scalar.activation(values[0][:, tb, :].rearrange("p (h d) -> p h d", h=HEADS),
                                         kv[:, :, 1, :], ACT.Copy,
                                         scale=roots[:, r, 4 + tb:5 + tb]).then_inc(emptied_by["act"], 1)
                if kind == "aturn":
                    tb = step[1]
                    n = l * NU + UNIT_AT[step]
                    for i in range(2):
                        act.wait_ge(unit_ready, n + 1 + i)
                        nc.scalar.activation(aqk[0:A_QK, i, :, tb * P:(tb + 1) * P],
                                             bank[0:A_QK, unit_bank(n + i), :].rearrange(
                                                 "p (h t) -> p h t", h=HEADS),
                                             ACT.Copy).then_inc(emptied_by["act"], 1)
                if kind == "mix":
                    k = step[1]
                    wait_gated(act, l, k)
                    nc.scalar.activation(mix[:, 0, k, :], gate[:, k, :], ACT.Copy).then_inc(mix_high, 1)
                if kind == "y01":
                    high(l * NG + NGI + 3)
                    for tb in range(NB):
                        square_y(l, tb, 0)
                if kind == "y":
                    square_y(l, step[1], 1)
                    if step[1] == 0:
                        high((l + 1) * NG)

        @block.vector
        def _(dve):
            steps = [0]

            def after(ins):
                steps[0] += 1
                ins.then_inc(vector_step, 1)
                dve.wait_ge(vector_step, steps[0])

            relus = [0]

            def mean_h(l, tb):
                r = ROOT_AT[l, ("hmean", tb)]
                dve.wait_ge(squares_summed, l * NB + tb + 1)
                if r >= 2:
                    dve.wait_ge(roots_ready, r - 1)
                nc.vector.tensor_scalar(means[:, r % 2, 0:1], sumsq[:, tb:tb + 1], 1.0 / DM, EPS, ALU.mult, ALU.add
                                        ).then_inc(means_ready, 1)

            def norm_h(l, tb):
                r = ROOT_AT[l, ("hmean", tb)]
                n = l * NU + UNIT_AT[("u", tb)]
                dve.wait_ge(roots_ready, r + 1)
                if tb == 0:
                    dve.wait_ge(gpre_loaded, 16 * (l + 1))
                if tb >= 2:
                    dve.wait_ge(unit_ready, l * NU + UNIT_AT[("u", tb - 2)] + 2)
                nc.vector.scalar_tensor_tensor(u[tb % 2][:], hX[:, tb, :], roots[:, r, 0:1], gpre[:], ALU.mult, ALU.mult
                                               ).then_inc(u_ready, 1)

            def low_u(l, tb):
                for half in range(2):
                    n = l * NU + UNIT_AT[("u", tb)] + half
                    dve.wait_ge(high_written, highs(n))
                    ks, ts = slice(4 * half, 4 * half + 4), slice(tb * P, (tb + 1) * P)
                    nc.vector.tensor_tensor(uT[:, 1, ks, ts], bank[:, unit_bank(n), :].rearrange("p (k t) -> p k t", k=4),
                                            uT[:, 0, ks, ts].bitcast(F32), ALU.subtract).then_inc(emptied_by["dve"], 1)

            after(nc.vector.memset(means[:], 1.0))

            def lambda_dots():
                pair = lamin[:].rearrange("p l (e t) d -> p l e t d", t=2)
                after(nc.vector.tensor_tensor(lampr[:], pair[:, :, :, 0, :], pair[:, :, :, 1, :], ALU.mult))
                nc.vector.tensor_reduce(lamdot[:], lampr[:], AX_X, ALU.add).then_inc(lam_dots, 1)

            def lambdas():
                dve.wait_ge(lam_exp, 1)
                after(nc.vector.tensor_tensor(neglam[:], lamdot[:, :, 1], lamdot[:, :, 0], ALU.subtract))
                for l in range(DEPTH):
                    after(nc.vector.tensor_scalar(neglam[:, l:l + 1], neglam[:, l:l + 1], -lam_init[l], None, ALU.add))
                    after(nc.vector.tensor_scalar(subln[:, l:l + 1], subln[:, l:l + 1], 0.5 * (1.0 - lam_init[l]), None,
                                                  ALU.mult))

            def select_round(r):
                q = SEL_BLOCKS[r // 16]
                row = select[:, POFF[q] - P:POFF[q] - P + WID[q]]
                after(nc.vector.max(best[:], row))
                after(nc.vector.match_replace(row, best[:], row, MARK))

            def normalise(l, j):
                dve.wait_ge(exp_done, l * NSJ + S_AT[j + 1])
                bufs = probs_buffers(j)
                i = j % 4
                if MAPS[j] == 2:
                    after(nc.vector.reciprocal(inv[:, i], sums[:, i]))
                    after(nc.vector.scalar_tensor_tensor(coef[:, i], inv[:, i, 1], neglam[:, l:l + 1], sums[:, i, 0],
                                                         ALU.mult, ALU.mult))
                    for q in range(NB):
                        sl = slice(POFF[q], POFF[q] + WID[q])
                        ins = nc.vector.scalar_tensor_tensor(probs[bufs[0]][:, sl], probs[bufs[1]][:, sl],
                                                             coef[:, i, q:q + 1], probs[bufs[0]][:, sl],
                                                             ALU.mult, ALU.add)
                else:
                    after(nc.vector.reciprocal(inv[:, i, 0], sums[:, i, 0]))
                    for q in range(NB):
                        sl = slice(POFF[q], POFF[q] + WID[q])
                        ins = nc.vector.tensor_scalar(probs[bufs[0]][:, sl], probs[bufs[0]][:, sl],
                                                      inv[:, i, 0, q:q + 1], None, ALU.mult)
                ins.then_inc(probs_ready, 1)

            for l, step in SEQUENCE:
                kind = step[0]
                if kind == "hmean":
                    mean_h(l, step[1])
                if kind == "hnorm":
                    norm_h(l, step[1])
                if (l, step) == (0, ("hnorm", 1)):
                    dve.wait_ge(w_high_done, 1)
                    w = WIDTH[0]
                    nc.vector.tensor_tensor(w_low[:, 0, :, 0:w], w_raw[:, 0, :, 0:w], w_high[:, 0, :, 0:w].bitcast(F32),
                                            ALU.subtract).then_inc(w_low_done, 1)
                if kind == "u":
                    low_u(l, step[1])
                if (l, step) == (0, ("unit", "cq", 1)):
                    dve.wait_ge(table_ready, 1)
                    nc.vector.tensor_copy(table[:, 0:512], bank[0:13, SCORE, :])
                    nc.vector.tensor_copy(table[:, 512:TABLE_W], bank[0:13, SCORE + 1, 0:TABLE_W - 512]
                                          ).then_inc(table_copied, 1)
                    dve.wait_ge(consts_loaded, 16 * N_CONSTS)
                    lambda_dots()
                if (l, step) == (0, ("unit", "qi", 1)):
                    lambdas()
                if kind == "unit" and UNIT_READER[UNIT_AT[step]] == "dve":
                    name, c = step[1:]
                    n = l * NU + UNIT_AT[step]
                    b = bank[:, unit_bank(n), :]
                    scale = {"qi": 1 / 16, "dq": DQK ** -0.5, "cqq": HD ** -0.5, "bq": HD ** -0.5}.get(name, 1.0)
                    dve.wait_ge(high_written, highs(n))
                    if name == "cq":
                        ins = nc.vector.tensor_tensor(kidx[32:64, :], b[96:128, :], kidx[0:32, :].bitcast(F32),
                                                      ALU.subtract)
                    elif name[0] == "g":
                        k = 2 * "abcd".index(name[1]) + c
                        ins = nc.vector.scalar_tensor_tensor(gate[:, k, :], gate[:, k, :], 1.0, b, ALU.add, ALU.mult)
                    else:
                        if step[1:] in STACKED:
                            s = STACKED.index(step[1:])
                            hi, lo = staging[:, s % 2, 0, :], staging[:, s % 2, 1, :]
                        else:
                            qk = cqk if name[0] == "c" else bqk
                            hi, lo = (qk[:, int(name[1] == "k"), part, c, :] for part in range(2))
                        ins = nc.vector.scalar_tensor_tensor(lo, b, scale, hi.bitcast(F32), ALU.mult, ALU.subtract)
                    ins.then_inc(emptied_by["dve"], 1)
                if kind == "idx":
                    h = step[1]
                    for q in SEL_BLOCKS:
                        row = select[:, POFF[q] - P:POFF[q] - P + WID[q]]
                        if h == 0:
                            dve.wait_ge(mask_loaded, 16)
                            wait_unit_emptied(dve, l * NU + UNIT_AT[("unit", "cv", NB - 1)])
                        before = mask[:, SEQ - WID[q]:SEQ] if h == 0 else row
                        dve.wait_ge(relu_done, relus[0] + 1)
                        if h > 0:
                            dve.wait_ge(index_added, relus[0] - 2)
                        nc.vector.scalar_tensor_tensor(row, probs[relus[0] % 4][:, 0:WID[q]], wi[:, q, h:h + 1],
                                                       before, ALU.mult, ALU.add).then_inc(index_added, 1)
                        relus[0] += 1
                if kind == "topk":
                    if step[1] == 0:
                        dve.wait_ge(index_added, relus[0])
                    for r in range(step[1], step[2]):
                        select_round(r)
                if kind == "topk" and step[2] == TOPK_ROUNDS:
                    nc.vector.tensor_scalar(select[:], select[:], 0.5 * MARK, NEG, ALU.is_gt, ALU.mult
                                            ).then_inc(select_done, 1)
                if kind == "scores":
                    j = step[1]
                    br, h = JOBS[j]
                    if br != "A":
                        dve.wait_ge(strips_loaded[h], 16 * (3 * l + BRANCHES.index(br) + 1))
                    if br == "C":
                        dve.wait_ge(bias_ready, l * HEADS + h + 1)
                    elif last_user(j) is not None:
                        dve.wait_ge(turn_ready, NB * (l * NJ + last_user(j) + 1))
                    for i in range(step[2], step[3]):
                        m, q = divmod(i, NB)
                        n = l * NS + NS_IDX + S_AT[j] + i
                        dve.wait_ge(scores_ready, n + 1)
                        sl = probs[probs_buffers(j)[m]][:, POFF[q]:POFF[q] + WID[q]]
                        bias = mask[:, SEQ - WID[q]:SEQ] if br == "A" else \
                            sl if br == "C" and q > 0 else strips[:, h, SEQ - WID[q]:SEQ]
                        nc.vector.tensor_tensor_reduce(sl, bank[:, SCORE + n % 3, 0:WID[q]], bias, -1.0, 3.0e38,
                                                       ALU.add, ALU.min, negmax[:, j % 4, m, q:q + 1]
                                                       ).then_inc(shifted, 1)
                if kind == "norm":
                    normalise(l, step[1])
                if kind == "pv":
                    j = step[1]
                    br, h = JOBS[j]
                    dve.wait_ge(pv_ready, l * NJ + j + 1)
                    if br == "D":
                        if h % 2 == 0 and (h > 0 or l > 0):
                            dve.wait_ge(unit_ready, (l if h else l - 1) * NU + UNIT_AT[("dnorm", 0 if h else 1)] + 1)
                        nc.vector.tensor_tensor(od[:, :, h % 2, :],
                                                bank[:, PV, 0:NB * HD].rearrange("p (t d) -> p t d", d=HD),
                                                inv[:, j % 4, 0, :].unsqueeze(2).to_broadcast([P, NB, HD]),
                                                ALU.mult).then_inc(pv_emptied, 1)
                    else:
                        k, half = 2 * "ABC".index(br) + h // 2, h % 2
                        g = gate[HD * half:HD * (half + 1), k, :]
                        nc.vector.scalar_tensor_tensor(g, bank[0:HD, PV, :], 0.5, g, ALU.mult, ALU.mult
                                                       ).then_inc(pv_emptied, 1)
                if kind == "dsquares":
                    r = ROOT_AT[l, step]
                    dve.wait_ge(pv_emptied, l * NJ + 2 * step[1] + 2)
                    after(nc.vector.tensor_tensor(odsq[:], od[:], od[:], ALU.mult))
                    after(nc.vector.tensor_reduce(dsum[:].rearrange("p (t h) -> p t h", h=2), odsq[:], AX_X, ALU.add))
                    nc.vector.tensor_scalar(means[:, r % 2, :], dsum[:], 1.0 / HD, EPS, ALU.mult, ALU.add
                                            ).then_inc(means_ready, 1)
                if kind == "dscale":
                    r = ROOT_AT[l, ("dsquares", step[1])]
                    dve.wait_ge(roots_ready, r + 1)
                    nc.vector.tensor_tensor(od[:], od[:],
                                            roots[:, r, :].rearrange("p (t h) -> p t h", h=2).unsqueeze(3)
                                            .to_broadcast([P, NB, 2, HD]), ALU.mult).then_inc(od_ready, 1)
                if kind == "dnorm":
                    n = l * NU + UNIT_AT[step]
                    k = 6 + step[1]
                    dve.wait_ge(unit_ready, n + 1)
                    nc.vector.scalar_tensor_tensor(gate[:, k, :], bank[:, unit_bank(n), :], subln[:, l:l + 1],
                                                   gate[:, k, :], ALU.mult, ALU.mult).then_inc(emptied_by["dve"], 1)
                if kind == "aup_head":
                    n = l * NU + UNIT_AT[step]
                    r = ROOT_AT[l, ("aup_head",)]
                    dve.wait_ge(a_loaded, 48 * (l + 1))
                    nc.vector.tensor_scalar(wuq[:, 0, :], wuq[:, 0, :], gq[:, l, 0:1], A_QK ** -0.5, ALU.mult, ALU.mult)
                    nc.vector.tensor_scalar(wuq[0:QL - P, 1, :], wuq[0:QL - P, 1, :], gq[0:QL - P, l, 1:2],
                                            A_QK ** -0.5, ALU.mult, ALU.mult)
                    nc.vector.tensor_scalar(wukv[:], wukv[:], gkv[:, l:l + 1], None, ALU.mult).then_inc(a_folded, 1)
                    dve.wait_ge(unit_ready, n + 1)
                    s8 = bank[:, unit_bank(n), 0:8]
                    after(nc.vector.tensor_scalar(means[:, r % 2, 0:4], s8[:, 0:4], 1.0 / QL, EPS, ALU.mult, ALU.add))
                    nc.vector.tensor_scalar(means[:, r % 2, 4:8], s8[:, 4:8], 1.0 / KVL, EPS, ALU.mult, ALU.add
                                            ).then_inc(means_ready, 1)
                    nc.vector.tensor_copy(coef[:, 0, 0:1], s8[:, 0:1]).then_inc(emptied_by["dve"], 1)
                    dve.wait_ge(unit_ready, n + 2)
                    after(nc.vector.tensor_copy(krx[:], bank[:, unit_bank(n + 1), 0:NB * A_ROPE].rearrange(
                        "p (t r) -> p t r", t=NB)))
                    hr = A_ROPE // 2
                    nc.vector.tensor_tensor(kr2[:, :, 0:hr], krx[:, :, hr:], ss[:, :, 0:hr], ALU.mult)
                    nc.vector.tensor_tensor(kr2[:, :, hr:], krx[:, :, 0:hr], ss[:, :, hr:], ALU.mult)
                    after(nc.vector.tensor_tensor(kr[:], krx[:], cc[:], ALU.mult))
                    nc.vector.tensor_tensor(kr[:], kr[:], kr2[:], ALU.add).then_inc(kr_ready, 1)
                    nc.vector.tensor_copy(coef[:, 0, 0:1], krx[:, 0, 0:1]).then_inc(emptied_by["dve"], 1)
                if kind == "aup":
                    tb = step[1]
                    n = l * NU + UNIT_AT[step]
                    r = ROOT_AT[l, ("aup_head",)]
                    t = tokq[tb % 2]
                    dve.wait_ge(roots_ready, r + 1)
                    dve.wait_ge(unit_ready, n + 1)
                    if tb >= 2:
                        dve.wait_ge(unit_ready, l * NU + UNIT_AT[("aturn", tb - 2)] + 1)
                    nc.vector.tensor_scalar(t[:].rearrange("p h d -> p (h d)"), bank[:, unit_bank(n), 0:HEADS * A_QK],
                                            roots[:, r, tb:tb + 1], None, ALU.mult).then_inc(emptied_by["dve"], 1)
                    wait_unit_emptied(dve, n)
                    rot = t[:, :, HD:A_QK]
                    hr = A_ROPE // 2
                    each = lambda tab, a, b: tab[:, tb, a:b].unsqueeze(1).to_broadcast([P, HEADS, b - a])
                    nc.vector.tensor_tensor(ropet[:, :, 0:hr], rot[:, :, hr:], each(ss, 0, hr), ALU.mult)
                    after(nc.vector.tensor_tensor(ropet[:, :, hr:], rot[:, :, 0:hr], each(ss, hr, A_ROPE), ALU.mult))
                    after(nc.vector.tensor_tensor(rot, rot, each(cc, 0, A_ROPE), ALU.mult))
                    nc.vector.tensor_tensor(rot, rot, ropet[:], ALU.add).then_inc(tokq_ready, 1)
                if kind == "mix":
                    k = step[1]
                    dve.wait_ge(mix_high, l * KC + MIX_ORDER.index(k) + 1)
                    nc.vector.tensor_tensor(mix[:, 1, k, :], gate[:, k, :], mix[:, 0, k, :].bitcast(F32),
                                            ALU.subtract).then_inc(mix_low, 1)
                if kind == "y":
                    tb = step[1]
                    r = ROOT_AT[l, step]
                    dve.wait_ge(y_squared, (l + 1) * NB + l * NB + tb + 1)
                    dve.wait_ge(roots_ready, r - 1)
                    after(nc.vector.tensor_tensor(dsum[:, 0:1], ysq[:, tb, 0:1], ysq[:, tb, 1:2], ALU.add))
                    nc.vector.tensor_scalar(means[:, r % 2, 0:1], dsum[:, 0:1], 1.0 / DM, EPS,
                                            ALU.mult, ALU.add).then_inc(means_ready, 1)
                if kind == "hupdate":
                    tb = step[1]
                    r = ROOT_AT[l, ("y", tb)]
                    if tb == 0:
                        dve.wait_ge(gpost_loaded, 16 * (l + 1))
                    nc.vector.tensor_tensor(yg[:, tb, :], bank[:, 2 * tb:2 * tb + 2, :].rearrange("p b c -> p (b c)"),
                                            gpost[:], ALU.mult).then_inc(y_emptied, 1)
                    dve.wait_ge(roots_ready, r + 1)
                    dve.wait_ge(y_emptied, l * NB + tb + 1)
                    dve.wait_ge(h_loaded[tb], 16 * (l + 2))
                    nc.vector.scalar_tensor_tensor(hX[:, tb, :], yg[:, tb, :], roots[:, r, 0:1], hX[:, tb, :],
                                                   ALU.mult, ALU.add).then_inc(h_updated, 1)

        @block.tensor
        def _(pe):
            def work_bank(n):
                before = n - 1
                while before >= 0 and unit_bank(before) != unit_bank(n):
                    before -= 1
                if before >= 0:
                    wait_unit_emptied(pe, before)
                return bank[:, unit_bank(n), :]

            def score_bank(l, i):
                n = l * NS + i
                if n >= 3:
                    ll, ii = divmod(n - 3, NS)
                    if ii < NS_IDX:
                        pe.wait_ge(relu_done, ll * NS_IDX + ii + 1)
                    else:
                        pe.wait_ge(shifted, ll * NSJ + ii - NS_IDX + 1)
                return bank[:, SCORE + n % 3, :]

            def turn_in(l, tb):
                n = l * NU + UNIT_AT[("u", tb)]
                pe.wait_ge(u_ready, l * NB + tb + 1)
                if l > 0 and tb == 0:
                    pe.wait_ge(y_emptied, (l - 1) * NB + 2)
                for half in range(2):
                    b = work_bank(n + half)
                    for k in range(4):
                        c = (4 * half + k) * P
                        ins = nc.tensor.transpose(b[:, k * P:(k + 1) * P], u[tb % 2][:, c:c + P], ident[:])
                    ins.then_inc(unit_ready, 1)

            def three(out_ap, lh, ll, rh, rl, start, stop):
                nc.tensor.matmul(out_ap, lh, rh, start=start, stop=False)
                nc.tensor.matmul(out_ap, lh, rl, start=False, stop=False)
                return nc.tensor.matmul(out_ap, ll, rh, start=False, stop=stop)

            def output(l, c, tb, first=0, last=KC):
                g = l * NG + NGI + c
                s = g % SLOTS
                pe.wait_ge(w_low_done, g + 1)
                ts = slice(tb * P, (tb + 1) * P)
                b = bank[:, 2 * tb + c // 2, (c % 2) * GO_W:(c % 2 + 1) * GO_W]
                for i in range(first, last):
                    k = MIX_ORDER[i]
                    if c == 0:
                        pe.wait_ge(mix_low, l * KC + i + 1)
                    ins = three(b, mix[:, 0, k, ts], mix[:, 1, k, ts], w_high[:, s, k, 0:GO_W],
                                w_low[:, s, k, 0:GO_W], i == 0, i == KC - 1)
                if last == KC:
                    ins.then_inc(y_ready, 1)

            pe.wait_ge(ident_loaded, 16)
            for l, step in SEQUENCE:
                kind = step[0]
                if kind == "u":
                    turn_in(l, step[1])
                if (l, step) == (0, ("unit", "cq", 0)):
                    pe.wait_ge(consts_loaded, 16 * N_CONSTS)
                    wait_unit_emptied(pe, UNIT_AT[("u", NB - 1)] + 1)
                    for a, b in ((0, 512), (512, TABLE_W)):
                        ins = nc.tensor.matmul(bank[0:13, SCORE + a // 512, 0:b - a], heads13[:], hot[:, a:b],
                                               start=True, stop=True)
                    ins.then_inc(table_ready, 1)
                if kind == "unit":
                    name, c = step[1:]
                    g = l * NG + GI[name]
                    s = g % SLOTS
                    n = l * NU + UNIT_AT[step]
                    token = GROUPS[GI[name]][2]
                    pe.wait_ge(w_low_done, g + 1)
                    wait_unit_emptied(pe, l * NU + UNIT_AT[("u", c if name == "cv" else NB - 1)] + 1)
                    b = work_bank(n)
                    w = WIDTH[GI[name]]
                    for k in range(KC):
                        if token:
                            ts = slice(c * P, (c + 1) * P)
                            ins = three(b[:, 0:w], uT[:, 0, k, ts], uT[:, 1, k, ts], w_high[:, s, k, 0:w],
                                        w_low[:, s, k, 0:w], k == 0, k == KC - 1)
                        else:
                            cs = slice(c * P, (c + 1) * P)
                            ins = three(b, w_high[:, s, k, cs], w_low[:, s, k, cs], uT[:, 0, k, :], uT[:, 1, k, :],
                                        k == 0, k == KC - 1)
                    ins.then_inc(unit_ready, 1)
                if kind == "idx":
                    h = step[1]
                    if h == 0:
                        wait_unit_emptied(pe, l * NU + UNIT_AT[("unit", "cq", 1)])
                        if l == 0:
                            pe.wait_ge(table_copied, 1)
                        else:
                            pe.wait_ge(y_emptied, l * NB)
                    if h % 4 == 0:
                        pe.wait_ge(stack_loaded[h // 4], 16 * STACK_DMAS * (l + 1))
                    for i, q in enumerate(SEL_BLOCKS):
                        b = score_bank(l, h * 3 + i)
                        nc.tensor.matmul(b[:, 0:WID[q]], qidx[0:96, h, q * P:(q + 1) * P], kidx[0:96, 0:WID[q]],
                                         start=True, stop=True).then_inc(scores_ready, 1)
                if kind == "scores":
                    j = step[1]
                    br, h = JOBS[j]
                    if step[2] == 0 and br == "D" and h % 2 == 0:
                        for s in (2 + h // 2, 4 + h // 2):
                            pe.wait_ge(stack_loaded[s], 16 * STACK_DMAS * (l + 1))
                    if br in "CB" and h == 0:
                        wait_unit_emptied(pe, l * NU + UNIT_AT[("unit", "ck" if br == "C" else "bk", 1)])
                    if br == "A" and h == 0:
                        wait_unit_emptied(pe, l * NU + UNIT_AT[("aturn", NB - 1)] + 1)
                    for i in range(step[2], step[3]):
                        m, q = divmod(i, NB)
                        b = score_bank(l, NS_IDX + S_AT[j] + i)[:, 0:WID[q]]
                        qs, ks = slice(q * P, (q + 1) * P), slice(0, WID[q])
                        if br == "D":
                            st = dqk[h // 2]
                            pair = 2 * (h % 2) + m
                            ins = nc.tensor.matmul(b, st[0:96, 0, pair, qs], st[0:96, 1, pair, ks],
                                                   start=True, stop=True)
                        elif br == "A":
                            ins = nc.tensor.matmul(b, aqk[0:A_QK, 0, h, qs], aqk[0:A_QK, 1, h, ks],
                                                   start=True, stop=True)
                        else:
                            qk = cqk if br == "C" else bqk
                            rows = slice(HD * (h % 2), HD * (h % 2) + HD)
                            ins = three(b, qk[rows, 0, 0, h // 2, qs], qk[rows, 0, 1, h // 2, qs],
                                        qk[rows, 1, 0, h // 2, ks], qk[rows, 1, 1, h // 2, ks], True, True)
                        ins.then_inc(scores_ready, 1)
                if kind == "turn":
                    j, kb = step[1:]
                    jj = l * NJ + j
                    if kb == 0:
                        pe.wait_ge(probs_ready, jj + 1)
                        if j == 0 and l > 0:
                            pe.wait_ge(y_emptied, l * NB)
                    buf = probs[probs_buffers(j)[0]]
                    t = jj * NB + kb
                    if t >= 2:
                        pe.wait_ge(turn_emptied, t - 1)
                    for q in range(kb, NB):
                        ins = nc.tensor.transpose(bank[:, TURN + t % 2, (q - kb) * P:(q - kb + 1) * P],
                                                  buf[:, POFF[q] + kb * P:POFF[q] + (kb + 1) * P], ident[:])
                    ins.then_inc(turn_ready, 1)
                if kind == "pv":
                    j = step[1]
                    jj = l * NJ + j
                    br, h = JOBS[j]
                    v = values[1] if br == "C" else values[0]
                    tr = turned[j % 2]
                    pe.wait_ge(turn_emptied, (jj + 1) * NB)
                    if jj > 0:
                        pe.wait_ge(pv_emptied, jj)
                    if h == 0:
                        ready = {"D": ("unit", "dv", NB - 1), "C": ("unit", "cv", NB - 1),
                                 "B": ("unit", "bv", NB - 1), "A": ("aup", NB - 1)}[br]
                        wait_unit_emptied(pe, l * NU + UNIT_AT[ready] + int(br == "A"))
                    hs = slice(HD * h, HD * (h + 1))
                    if br == "D":
                        for q in range(NB):
                            for kb in range(q + 1):
                                a = TOFF[kb] + (q - kb) * P
                                ins = nc.tensor.matmul(bank[:, PV, HD * q:HD * (q + 1)], tr[:, a:a + P], v[:, kb, hs],
                                                       start=kb == 0, stop=kb == q)
                    else:
                        for kb in range(NB):
                            ins = nc.tensor.matmul(bank[0:HD, PV, kb * P:SEQ], v[:, kb, hs],
                                                   tr[:, TOFF[kb]:TOFF[kb] + P * (NB - kb)],
                                                   start=kb == 0, stop=kb == NB - 1)
                    ins.then_inc(pv_ready, 1)
                if kind == "dnorm":
                    n = l * NU + UNIT_AT[step]
                    pe.wait_ge(od_ready, 2 * l + step[1] + 1)
                    b = work_bank(n)
                    for tb in range(NB):
                        ins = nc.tensor.transpose(b[:, tb * P:(tb + 1) * P],
                                                  od[:, tb].rearrange("p h d -> p (h d)"), ident[:])
                    ins.then_inc(unit_ready, 1)
                if kind == "aup_head":
                    n = l * NU + UNIT_AT[step]
                    pe.wait_ge(lat_squared, l + 1)
                    b = work_bank(n)
                    for tb in range(NB):
                        ts = slice(tb * P, (tb + 1) * P)
                        nc.tensor.matmul(b[:, tb:tb + 1], sq[:, 0, ts], ones[:], start=True, stop=False)
                        nc.tensor.matmul(b[:, tb:tb + 1], sq[0:64, 1, ts], ones[0:64, :], start=False, stop=True)
                        ins = nc.tensor.matmul(b[:, 4 + tb:5 + tb], sq[:, 2, ts], ones[:], start=True, stop=True)
                    ins.then_inc(unit_ready, 1)
                    b = work_bank(n + 1)
                    for tb in range(NB):
                        ins = nc.tensor.transpose(b[:, tb * A_ROPE:(tb + 1) * A_ROPE],
                                                  latq[64:96, 1, tb * P:(tb + 1) * P], ident[64:96, 64:96])
                    ins.then_inc(unit_ready, 1)
                if kind == "aup":
                    tb = step[1]
                    ts = slice(tb * P, (tb + 1) * P)
                    n = l * NU + UNIT_AT[step]
                    pe.wait_ge(a_folded, l + 1)
                    b = work_bank(n)[:, 0:HEADS * A_QK]
                    nc.tensor.matmul(b, latq[:, 0, ts], wuq[:, 0, :], start=True, stop=False)
                    nc.tensor.matmul(b, latq[0:64, 1, ts], wuq[0:64, 1, :], start=False, stop=True
                                     ).then_inc(unit_ready, 1)
                    b = work_bank(n + 1)
                    nc.tensor.matmul(b, latkv[:, ts], wukv[:], start=True, stop=True).then_inc(unit_ready, 1)
                if kind == "aturn":
                    tb = step[1]
                    n = l * NU + UNIT_AT[step]
                    for i, tok in enumerate((tokq, tokk)):
                        if i == 0:
                            pe.wait_ge(tokq_ready, l * NB + tb + 1)
                        else:
                            wait_unit_emptied(pe, l * NU + UNIT_AT[("aup", tb)] + 1)
                        b = work_bank(n + i)
                        for h in range(HEADS):
                            ins = nc.tensor.transpose(b[0:A_QK, h * P:(h + 1) * P], tok[tb % 2][:, h, :], ident[:])
                        ins.then_inc(unit_ready, 1)
                if kind == "ya":
                    wait_unit_emptied(pe, l * NU + NU - 1)
                    pe.wait_ge(shifted, (l + 1) * NSJ)
                    output(l, 0, step[1], 0, EARLY)
                if kind == "y01":
                    pe.wait_ge(turn_emptied, (l + 1) * NJ * NB)
                    for tb in range(NB):
                        output(l, 0, tb, EARLY if tb < 3 else 0, KC - 1)
                    for tb in range(NB):
                        output(l, 0, tb, KC - 1, KC)
                    for tb in range(NB):
                        output(l, 1, tb)
                if kind == "y":
                    if step[1] == NB - 1:
                        pe.wait_ge(pv_emptied, (l + 1) * NJ)
                    for c in range(2, NGO):
                        output(l, c, step[1])


_INS = ["x", "w_in", "w_out", "norm_pre", "norm_post", "mla_q_norm", "mla_kv_norm", "mla_w_uq", "mla_w_ukv",
        "diff_lambda", "diff_subln", "rel_bias"]


def bucket_of(n):
    exact = BUCKETS // 2
    nf = np.maximum(n, exact).astype(np.float32)
    large = exact + (np.log(nf / np.float32(exact)) / np.float32(np.log(2048 / exact))
                     * np.float32(BUCKETS - exact)).astype(np.int32)
    return np.where(n < exact, n, np.minimum(large, BUCKETS - 1))


def constants():
    rel = SEQ - 1 - np.arange(TABLE_W)
    onehot = np.zeros((34, TABLE_W), np.float32)
    for c, r in enumerate(rel):
        if r >= 0:
            onehot[bucket_of(np.array([r]))[0], c] = 1.0
            times = int(r <= 128) + int(r % 4 == 0) + int(r % 16 == 0)
            onehot[33, c] = np.log(times) if times else NEG
        else:
            onehot[32, c] = NEG
    headrows = np.zeros((34, 13), np.float32)
    headrows[32, :] = 1.0
    headrows[33, 0:4] = 1.0
    inv = (np.float32(10000.0) ** (-np.arange(0, A_ROPE, 2, dtype=np.float32) / np.float32(A_ROPE))).astype(np.float32)
    ang = np.arange(SEQ, dtype=np.float32)[:, None] * inv[None, :]
    cos, sin = np.cos(ang), np.sin(ang)
    return {"onehot": onehot, "headrows": headrows,
            "rope_cc": np.concatenate([cos, cos], 1).astype(np.float32),
            "rope_ss": np.concatenate([-sin, sin], 1).astype(np.float32),
            "ident": np.eye(P, dtype=np.float32)}


def kernel(**inputs):
    from concourse import bacc
    from concourse.bass_utils import run_bass_kernel_spmd

    nc = bacc.Bacc("TRN2", target_bir_lowering=False, num_devices=1)
    arrays, args = {}, []
    for name, a in [(n, inputs[n]) for n in _INS] + list(constants().items()):
        a = np.ascontiguousarray(a)
        arrays[f"in_{name}"] = a
        args.append(nc.dram_tensor(f"in_{name}", a.shape, mybir.dt.from_np(a.dtype), kind="ExternalInput").ap())
    args.append(nc.dram_tensor("out_h", (1, SEQ, DM), F32, kind="ExternalOutput").ap())
    trunk(nc, *args)
    r = run_bass_kernel_spmd(nc, [arrays], core_ids=[0])
    return r.results[0]["out_h"]
```
